# Optimizing a Trainium2 kernel written in Bass

```python
import jax
import jax.numpy as jnp
from jax import lax

D_MODEL = 1024
BATCH = 1
SEQ = 512
DEPTH = 1

N_ATTN_HEADS = 8
HEAD_DIM = 64
ATTN_WIDTH = N_ATTN_HEADS * HEAD_DIM
MOBA_BLOCK = 256
MOBA_TOPK = 3
MOBA_Q_BLOCK = 64
N_SGU_GROUPS = 8
SGU_GROUP_DIM = 64
SGU_WIDTH = N_SGU_GROUPS * SGU_GROUP_DIM
SGU_CHUNK = 128
D_FF = 2816
CONV_WIDTH = 3
N_MOD = 6
EPS = 1e-6
IN_WIDTH = 3 * ATTN_WIDTH + 2 * SGU_WIDTH + 2 * D_MODEL

kernel_name = 'hybrid_moba_gmlp_convffn_adaln'

def rms_norm(x, g):
    xf = x.astype(jnp.float32)
    y = xf * lax.rsqrt(jnp.mean(xf * xf, axis=-1, keepdims=True) + EPS)
    return (y * g.astype(jnp.float32)).astype(x.dtype)

def modulate(h, shift, scale):
    return h * (1 + scale[:, None, :]) + shift[:, None, :]

def moba_attention(q, k, v):
    b, s, h, dh = q.shape
    s_pad = -(-s // MOBA_BLOCK) * MOBA_BLOCK
    pad = ((0, 0), (0, s_pad - s), (0, 0), (0, 0))
    nb = s_pad // MOBA_BLOCK
    q = jnp.pad(q * dh ** -0.5, pad).transpose(0, 2, 1, 3)
    kb = jnp.pad(k, pad).transpose(0, 2, 1, 3).reshape(b, h, nb, MOBA_BLOCK, dh)
    vb = jnp.pad(v, pad).transpose(0, 2, 1, 3).reshape(b, h, nb, MOBA_BLOCK, dh)
    topk = min(MOBA_TOPK, nb)
    k_mean = jnp.mean(kb.astype(jnp.float32), axis=3)
    route = jnp.einsum('bhsd,bhnd->bhsn', q.astype(jnp.float32), k_mean)
    q_block = jnp.arange(s_pad) // MOBA_BLOCK
    fully_past = jnp.arange(nb)[None, :] < q_block[:, None]
    route = jnp.where(fully_past, route, -jnp.inf)
    _, sel = lax.top_k(route, topk)
    nq = s_pad // MOBA_Q_BLOCK
    q_c = q.reshape(b, h, nq, MOBA_Q_BLOCK, dh).transpose(2, 0, 1, 3, 4)
    sel_c = sel.reshape(b, h, nq, MOBA_Q_BLOCK, topk).transpose(2, 0, 1, 3, 4)
    bi = jnp.arange(b)[:, None, None, None]
    hi = jnp.arange(h)[None, :, None, None]

    def query_block(args):
        ci, qc, selc = args
        pos_q = ci * MOBA_Q_BLOCK + jnp.arange(MOBA_Q_BLOCK)
        blk = (ci * MOBA_Q_BLOCK) // MOBA_BLOCK
        k_sel = kb[bi, hi, selc]
        v_sel = vb[bi, hi, selc]
        s_sel = jnp.einsum('bhqd,bhqnkd->bhqnk', qc, k_sel).astype(jnp.float32)
        valid = jnp.arange(topk)[None, :] < (pos_q // MOBA_BLOCK)[:, None]
        s_sel = jnp.where(valid[None, None, :, :, None], s_sel, -jnp.inf)
        k_own = lax.dynamic_index_in_dim(kb, blk, axis=2, keepdims=False)
        v_own = lax.dynamic_index_in_dim(vb, blk, axis=2, keepdims=False)
        s_own = jnp.einsum('bhqd,bhkd->bhqk', qc, k_own).astype(jnp.float32)
        pos_k = blk * MOBA_BLOCK + jnp.arange(MOBA_BLOCK)
        s_own = jnp.where(pos_k[None, :] <= pos_q[:, None], s_own, -jnp.inf)
        scores = jnp.concatenate(
            [s_sel.reshape(b, h, MOBA_Q_BLOCK, topk * MOBA_BLOCK), s_own], axis=-1)
        p = jax.nn.softmax(scores, axis=-1).astype(v.dtype)
        p_sel = p[..., :topk * MOBA_BLOCK].reshape(b, h, MOBA_Q_BLOCK, topk, MOBA_BLOCK)
        p_own = p[..., topk * MOBA_BLOCK:]
        return (jnp.einsum('bhqnk,bhqnkd->bhqd', p_sel, v_sel)
                + jnp.einsum('bhqk,bhkd->bhqd', p_own, v_own))

    out = lax.map(query_block, (jnp.arange(nq), q_c, sel_c))
    out = out.transpose(1, 0, 3, 2, 4).reshape(b, s_pad, h * dh)
    return out[:, :s]

def spatial_gating(u, v, g_v, w_s, b_s):
    b, s, _ = v.shape
    v = rms_norm(v, g_v).reshape(b, s // SGU_CHUNK, SGU_CHUNK, N_SGU_GROUPS, SGU_GROUP_DIM)
    causal = jnp.tril(jnp.ones((SGU_CHUNK, SGU_CHUNK), dtype=bool))
    w = jnp.where(causal[None], w_s, 0)
    mixed = jnp.einsum('gij,bnjgc->bnigc', w, v) + b_s.T[None, None, :, :, None]
    return u * mixed.reshape(b, s, SGU_WIDTH)

def causal_dwconv(h, w, bias):
    s = h.shape[1]
    hp = jnp.pad(h, ((0, 0), (CONV_WIDTH - 1, 0), (0, 0)))
    out = bias + w[CONV_WIDTH - 1] * h
    for i in range(CONV_WIDTH - 1):
        out = out + w[i] * hp[:, i:i + s]
    return out

def setup_inputs(seed: int = 0) -> dict:
    key = jax.random.key(seed)
    ks = jax.random.split(key, 18)

    def nrm(k, shape, scale):
        return jax.random.normal(k, shape, jnp.float32) * scale

    L = DEPTH
    return {
        'x': nrm(ks[0], (BATCH, SEQ, D_MODEL), 1.0),
        'c': nrm(ks[1], (BATCH, D_MODEL), 1.0),
        'w_mod': nrm(ks[2], (L, D_MODEL, N_MOD * D_MODEL), 0.5 * D_MODEL ** -0.5),
        'b_mod': nrm(ks[3], (L, N_MOD * D_MODEL), 0.02),
        'g_mix': 1.0 + nrm(ks[4], (L, D_MODEL), 0.05),
        'w_in': nrm(ks[5], (L, D_MODEL, IN_WIDTH), D_MODEL ** -0.5),
        'g_sgu': 1.0 + nrm(ks[6], (L, SGU_WIDTH), 0.05),
        'w_sgu_s': nrm(ks[7], (L, N_SGU_GROUPS, SGU_CHUNK, SGU_CHUNK), SGU_CHUNK ** -0.5),
        'b_sgu_s': 1.0 + nrm(ks[8], (L, N_SGU_GROUPS, SGU_CHUNK), 0.1),
        'w_attn_br': nrm(ks[9], (L, ATTN_WIDTH, D_MODEL), ATTN_WIDTH ** -0.5),
        'w_sgu_br': nrm(ks[10], (L, SGU_WIDTH, D_MODEL), SGU_WIDTH ** -0.5),
        'w_out': nrm(ks[11], (L, D_MODEL, D_MODEL), D_MODEL ** -0.5),
        'g_ffn': 1.0 + nrm(ks[12], (L, D_MODEL), 0.05),
        'w_up': nrm(ks[13], (L, D_MODEL, 2 * D_FF), D_MODEL ** -0.5),
        'w_conv': nrm(ks[14], (L, CONV_WIDTH, 2 * D_FF), CONV_WIDTH ** -0.5),
        'b_conv': nrm(ks[15], (L, 2 * D_FF), 0.02),
        'w_down': nrm(ks[16], (L, D_FF, D_MODEL), D_FF ** -0.5),
        'g_final': 1.0 + nrm(ks[17], (D_MODEL,), 0.05),
    }

def reference(x, c, w_mod, b_mod, g_mix, w_in, g_sgu, w_sgu_s, b_sgu_s, w_attn_br,
              w_sgu_br, w_out, g_ffn, w_up, w_conv, b_conv, w_down, g_final):
    b, s, _ = x.shape
    a3 = 3 * ATTN_WIDTH
    splits = [ATTN_WIDTH, 2 * ATTN_WIDTH, a3, a3 + SGU_WIDTH, a3 + 2 * SGU_WIDTH,
              a3 + 2 * SGU_WIDTH + D_MODEL]
    c_act = jax.nn.silu(c)
    for l in range(DEPTH):
        mod = c_act @ w_mod[l] + b_mod[l]
        shift_m, scale_m, gate_m, shift_f, scale_f, gate_f = jnp.split(mod, N_MOD, axis=-1)

        h = modulate(rms_norm(x, g_mix[l]), shift_m, scale_m)
        q, k, v, u, vs, gate_a, gate_s = jnp.split(h @ w_in[l], splits, axis=-1)
        head_shape = (b, s, N_ATTN_HEADS, HEAD_DIM)
        y_attn = moba_attention(q.reshape(head_shape), k.reshape(head_shape),
                                v.reshape(head_shape)) @ w_attn_br[l]
        y_sgu = spatial_gating(jax.nn.gelu(u), jax.nn.gelu(vs), g_sgu[l],
                               w_sgu_s[l], b_sgu_s[l]) @ w_sgu_br[l]
        merged = jax.nn.sigmoid(gate_a) * y_attn + jax.nn.sigmoid(gate_s) * y_sgu
        x = x + gate_m[:, None, :] * (merged @ w_out[l])

        h = modulate(rms_norm(x, g_ffn[l]), shift_f, scale_f)
        act, lin = jnp.split(causal_dwconv(h @ w_up[l], w_conv[l], b_conv[l]), 2, axis=-1)
        x = x + gate_f[:, None, :] * ((jax.nn.silu(act) * lin) @ w_down[l])
    return rms_norm(x, g_final)


_drawn_inputs = setup_inputs


def setup_inputs(seed=0):
    import zlib

    import numpy as np

    out = dict(_drawn_inputs(seed))
    spreads = {}
    factors = {'b_mod': 2.904,
     'g_mix': 6.102,
     'g_sgu': 8.0,
     'b_sgu_s': 5.113,
     'g_ffn': 4.069,
     'b_conv': 8.0}
    for name, (base, spread) in spreads.items():
        noise = np.random.default_rng([zlib.crc32(name.encode()), seed]).standard_normal(out[name].shape)
        drawn = base * np.exp(spread * noise) if base else spread * noise
        out[name] = jnp.asarray(drawn.astype(out[name].dtype))
    for name, factor in factors.items():
        out[name] = (out[name] * factor).astype(out[name].dtype)
    return out
```

```python
from contextlib import ExitStack

import concourse.bass as bass
from concourse import mybir

P = 128
D_MODEL, SEQ, HEADS, HEAD_DIM = 1024, 512, 8, 64
WIDTH = HEADS * HEAD_DIM
GROUPS = 8
D_FF = 2816
EPS = 1e-6
KC = D_MODEL // P
WC = WIDTH // P
FC = D_FF // P
TT = SEQ // P

T_VS, T_V, T_Q, T_K, T_U = 0, 4, 8, 12, 16
T_GATES = 20
T_BRANCH = T_GATES + 2 * KC
T_OUT = T_BRANCH + KC
T_UP = T_OUT + KC
T_DOWN = T_UP + 2 * FC
UNITS, DOWN_UNITS = 8, FC // 2
TILE, DOWN_TILE = UNITS * P, DOWN_UNITS * P
SLOTS = 4
N_DOWN = 2 * KC

C_C = 0
C_BMOD = C_C + KC
C_GMIX = C_BMOD + 6 * KC
C_GFFN = C_GMIX + KC
C_GFIN = C_GFFN + KC
C_WCONV = C_GFIN + KC
C_BCONV = C_WCONV + 3 * 2 * FC
N_COLS = C_BCONV + 2 * FC
SHIFT_M, SCALE_M, GATE_M, SHIFT_F, SCALE_F, GATE_F = (KC * n for n in range(6))
MOD_ORDER = [2, 3, 0, 1, 4, 5, 6, 7, 8, 9, 10, 11]
EARLY = 4
MOD_BUFS = 4
ACCS = 4

MASKED = -3.0e38
F32 = mybir.dt.float32
F32R = mybir.dt.float32r
BF16 = mybir.dt.bfloat16
ALU = mybir.AluOpType
ACT = mybir.ActivationFunctionType


def decoder_layer(nc, xT, cols_in, w_mod, tiles, down_tiles, w_sgu, g_sgu, b_sgu, out):
    with ExitStack() as ctx:
        def sem(name):
            return ctx.enter_context(nc.semaphore(name))

        def held(scope):
            return lambda name, shape, dt=F32: scope.enter_context(nc.sbuf_tensor(name, shape, dt))

        sb = held(ctx)
        x = sb("x", [P, KC, SEQ])
        h_hi = sb("h_hi", [P, KC, SEQ], F32R)
        h_lo = sb("h_lo", [P, KC, SEQ], F32R)
        raw = sb("raw", [P, SLOTS * TILE])
        w_hi = sb("w_hi", [P, SLOTS * TILE], F32R)
        w_lo = sb("w_lo", [P, SLOTS * TILE], F32R)
        cols = sb("cols", [P, N_COLS])
        c_act = sb("c_act", [P, KC])
        mod = sb("mod", [P, 6 * KC])
        gain = sb("gain", [P, 2, KC])
        small = sb("small", [P, 8, TT])
        ident = sb("ident", [P, P])
        ones = sb("ones", [P, P])
        mask = sb("mask", [P, SEQ], BF16)
        work = sb("work", [P, 2, SEQ])
        squares = sb("squares", [P, 2, SEQ])
        sum_sq = sb("sum_sq", [P, SEQ])
        diag = sb("diag", [P, SEQ])
        bank = [ctx.enter_context(nc.psum_tensor(f"bank{n}", [P, 512], F32)) for n in range(8)]

        with ExitStack() as mixing:
            sb = held(mixing)
            v = sb("v", [P, TT, WIDTH])
            qT = sb("qT", [P, WC, SEQ])
            kT = sb("kT", [P, WC, SEQ])
            with ExitStack() as early:
                sb = held(early)
                vs = sb("vs", [P, TT, WIDTH])
                mix = sb("mix", [P, WC, SEQ])
                u = sb("u", [P, 2, SEQ])
                w_spatial = sb("w_spatial", [P, GROUPS, P])
                g_row = sb("g_row", [P, WIDTH])
                b_row = sb("b_row", [P, WC, P])
                mod_w = sb("mod_w", [P, MOD_BUFS, 4, 512])
                mod_acc = sb("mod_acc", [P, ACCS, 512])
                mod_row = sb("mod_row", [P, 512])
                x_rstd = sb("x_rstd", [P, KC, SEQ])
            with ExitStack() as late:
                sb = held(late)
                gates = sb("gates", [P, 2 * KC, SEQ])
                attn_hi = sb("attn_hi", [P, WC, SEQ], F32R)
                attn_lo = sb("attn_lo", [P, WC, SEQ], F32R)
                sgu_hi = sb("sgu_hi", [P, WC, SEQ], F32R)
                sgu_lo = sb("sgu_lo", [P, WC, SEQ], F32R)
                q_hi = sb("q_hi", [P, SEQ], F32R)
                q_lo = sb("q_lo", [P, SEQ], F32R)
                k_hi = sb("k_hi", [P, SEQ], F32R)
                k_lo = sb("k_lo", [P, SEQ], F32R)
                v_pair = sb("v_pair", [P, TT, P])
                probs = sb("probs", [P, 2, SEQ])
                probsT = sb("probsT", [P, TT, SEQ])
        with ExitStack() as mlp:
            sb = held(mlp)
            g_hi = sb("g_hi", [P, FC, SEQ], F32R)
            g_lo = sb("g_lo", [P, FC, SEQ], F32R)
            conv_act = sb("conv_act", [P, 2, SEQ])
            conv_lin = sb("conv_lin", [P, 2, SEQ])
            glu = sb("glu", [P, 2, SEQ])

        x_landed = sem("x_landed")
        cols_landed = sem("cols_landed")
        sgu_landed = sem("sgu_landed")
        mod_landed = [sem(f"mod_landed{n}") for n in range(2 * EARLY)]
        raw_landed = [sem(f"raw_landed{n}") for n in range(SLOTS)]
        out_landed = sem("out_landed")
        consts_built = sem("consts_built")
        pool_order = sem("pool_order")
        spatial_masked = sem("spatial_masked")
        hi_ready = sem("hi_ready")
        lo_ready = sem("lo_ready")
        tile_done = sem("tile_done")
        c_ready = sem("c_ready")
        mod_half_summed = sem("mod_half_summed")
        mod_half_multiplied = sem("mod_half_multiplied")
        mod_row_ready = sem("mod_row_ready")
        mod_summed = sem("mod_summed")
        mod_in_bank = sem("mod_in_bank")
        mod_ready = sem("mod_ready")
        squared = sem("squared")
        square_added = sem("square_added")
        stats_done = sem("stats_done")
        mean_ready = sem("mean_ready")
        root_ready = sem("root_ready")
        diag_ready = sem("diag_ready")
        rstd_spread = sem("rstd_spread")
        normed = sem("normed")
        h_hi_ready = sem("h_hi_ready")
        h_ready = sem("h_ready")
        vs_ready = sem("vs_ready")
        v_ready = sem("v_ready")
        proj_ready = sem("proj_ready")
        vs_mean_ready = sem("vs_mean_ready")
        vs_root_ready = sem("vs_root_ready")
        vs_normed = sem("vs_normed")
        spatial_done = sem("spatial_done")
        mix_ready = sem("mix_ready")
        gated = sem("gated")
        sgu_hi_ready = sem("sgu_hi_ready")
        sgu_ready = sem("sgu_ready")
        pair_hi = sem("pair_hi")
        pair_lo = sem("pair_lo")
        v_staged = sem("v_staged")
        scores_done = sem("scores_done")
        scores_masked = sem("scores_masked")
        scores_taken = sem("scores_taken")
        exp_done = sem("exp_done")
        probs_ready = sem("probs_ready")
        probs_turned = sem("probs_turned")
        probsT_ready = sem("probsT_ready")
        head_done = sem("head_done")
        attn_hi_ready = sem("attn_hi_ready")
        attn_ready = sem("attn_ready")
        gate_ready = sem("gate_ready")
        branch_read = sem("branch_read")
        merged = sem("merged")
        merged_hi = sem("merged_hi")
        merged_ready = sem("merged_ready")
        mixed_in = sem("mixed_in")
        conv_begun = sem("conv_begun")
        conv_done = sem("conv_done")
        silu_done = sem("silu_done")
        glu_ready = sem("glu_ready")
        g_hi_ready = sem("g_hi_ready")
        g_ready = sem("g_ready")
        down_added = sem("down_added")
        dve_order = sem("dve_order")
        out_ready = sem("out_ready")

        mod_view = w_mod.rearrange("(k p) n -> p k n", p=P)
        out_view = out.rearrange("(c p) t -> p c t", p=P)

        early_bufs = [mod_w[:, n] for n in range(MOD_BUFS)] + [v, qT, kT, mix]

        def mod_half(n):
            return early_bufs[n] if n < 2 * EARLY else mod_w[:, n % MOD_BUFS]

        def wait_mod_landed(engine, n):
            if n < 2 * EARLY:
                engine.wait_ge(mod_landed[n], 16)
            else:
                engine.wait_ge(mod_landed[n % MOD_BUFS], 16 * (n // MOD_BUFS))

        def raw_slot(tile):
            return raw[:, tile % SLOTS * TILE:(tile % SLOTS + 1) * TILE]

        def part_slot(part, slot):
            return part[:, slot * TILE:(slot + 1) * TILE]

        def down_slot(part, n):
            return part[:, n % 2 * 2 * TILE:n % 2 * 2 * TILE + DOWN_TILE]

        block = ctx.enter_context(nc.Block())

        @block.sync
        def _(sp):
            def load_mod_half(n):
                if n >= 2 * EARLY + MOD_BUFS:
                    sp.wait_ge(mod_half_summed, n - MOD_BUFS - EARLY + 1)
                elif n >= 2 * EARLY:
                    sp.wait_ge(mod_half_multiplied if n % 2 else mod_half_summed, (n - 2 * EARLY) // 2 + 1)
                g, rows = MOD_ORDER[n // 2], n % 2 * 4
                sp.dma_start(mod_half(n)[:], mod_view[:, rows:rows + 4, g * 512:(g + 1) * 512]) \
                    .then_inc(mod_landed[n if n < 2 * EARLY else n % MOD_BUFS], 16)

            def load_tile(t):
                if t >= SLOTS:
                    sp.wait_ge(lo_ready, t - SLOTS + 1)
                sp.dma_start(raw_slot(t), tiles[t]).then_inc(raw_landed[t % SLOTS], 16)

            sp.dma_start(cols[:], cols_in).then_inc(cols_landed, 16)
            sp.dma_start(x[:], xT.rearrange("(c p) t -> p c t", p=P)).then_inc(x_landed, 16)
            for n in range(2 * EARLY):
                load_mod_half(n)
            for t in range(SLOTS):
                load_tile(t)
            sp.dma_start(w_spatial[:], w_sgu).then_inc(sgu_landed, 16)
            sp.dma_start(g_row[:], bass.AP(tensor=g_sgu.tensor, offset=0, ap=[[0, P], [1, WIDTH]])) \
                .then_inc(sgu_landed, 16)
            for half in range(2):
                sp.dma_start(b_row[64 * half:64 * half + 64],
                             bass.AP(tensor=b_sgu.tensor, offset=half * P, ap=[[0, 64], [2 * P, WC], [1, P]])) \
                    .then_inc(sgu_landed, 16)
            for t in range(SLOTS, 2 * SLOTS):
                load_mod_half(t + SLOTS)
                load_tile(t)
            for t in range(2 * SLOTS, 2 * SLOTS + 6):
                load_tile(t)
                load_mod_half(2 * t - 4)
                load_mod_half(2 * t - 3)
            for t in range(2 * SLOTS + 6, 4 * SLOTS):
                load_tile(t)
            with sp.Fori(4, T_DOWN // SLOTS) as i:
                for s in range(SLOTS):
                    sp.wait_ge(lo_ready, SLOTS * i + s - SLOTS + 1)
                    sp.dma_start(raw_slot(s), tiles[bass.ds(SLOTS * i + s, 1)].rearrange("a p n -> p (a n)")) \
                        .then_inc(raw_landed[s], 16)
            for n in range(2):
                sp.wait_ge(lo_ready, T_DOWN - 2 + 2 * n)
                sp.dma_start(down_slot(raw, n), down_tiles[n]).then_inc(raw_landed[2 * n], 16)
            with sp.Fori(1, N_DOWN // 2) as i:
                for n in range(2):
                    sp.wait_ge(lo_ready, T_DOWN + 2 * i + n - 1)
                    sp.dma_start(down_slot(raw, n), down_tiles[bass.ds(2 * i + n, 1)].rearrange("a p n -> p (a n)")) \
                        .then_inc(raw_landed[2 * n], 16)
            for c in range(KC):
                sp.wait_ge(out_ready, c + 1)
                sp.dma_start(out_view[:, c], x[:, c]).then_inc(out_landed, 16)
            sp.wait_ge(out_landed, 16 * KC)

        @block.gpsimd
        def _(pool):
            pool.memset(ones[:], 1.0).then_inc(pool_order, 1)
            pool.memset(mask[:], 0.0).then_inc(pool_order, 1)
            pool.wait_ge(pool_order, 2)
            pool.affine_select(out=ident[:], in_=ones[:], compare_op=ALU.is_equal, fill=0.0, base=0,
                               pattern=[[-1, P]], channel_multiplier=1).then_inc(consts_built, 1)
            pool.affine_select(out=mask[:], in_=mask[:], compare_op=ALU.is_ge, fill=MASKED, base=3 * P,
                               pattern=[[-1, SEQ]], channel_multiplier=1).then_inc(consts_built, 1)
            pool.wait_ge(sgu_landed, 64)
            pool.affine_select(out=w_spatial[:], in_=w_spatial[:], compare_op=ALU.is_ge, fill=0.0, base=0,
                               pattern=[[0, GROUPS], [1, P]], channel_multiplier=-1).then_inc(spatial_masked, 1)
            with pool.Fori(0, T_DOWN // SLOTS) as i:
                for s in range(SLOTS):
                    pool.wait_ge(hi_ready, SLOTS * i + s + 1)
                    pool.tensor_tensor(part_slot(w_lo, s), raw_slot(s), part_slot(w_hi, s).bitcast(F32),
                                       ALU.subtract).then_inc(lo_ready, 1)
            with pool.Fori(0, N_DOWN // 2) as i:
                for n in range(2):
                    pool.wait_ge(hi_ready, T_DOWN + 2 * i + n + 1)
                    pool.tensor_tensor(down_slot(w_lo, n), down_slot(raw, n), down_slot(w_hi, n).bitcast(F32),
                                       ALU.subtract).then_inc(lo_ready, 1)

        @block.scalar
        def _(act):
            def round_tile(t):
                s = t % SLOTS
                act.wait_ge(raw_landed[s], 16 * (t // SLOTS + 1))
                act.copy(part_slot(w_hi, s), raw_slot(s)).then_inc(hi_ready, 1)

            def square_chunks(chunk, ready, first, at):
                act.wait_ge(ready, at)
                act.wait_ge(square_added, first + 1)
                act.activation(squares[:, chunk % 2], x[:, chunk], ACT.Square).then_inc(squared, 1)

            act.sem_inc(probsT_ready, 2)
            act.sem_inc(gate_ready, 2)
            act.wait_ge(cols_landed, 16)
            act.activation(c_act[:], cols[:, C_C:C_C + KC], ACT.Silu).then_inc(c_ready, 1)
            act.wait_ge(x_landed, 16)
            for c in range(KC):
                square_chunks(c, x_landed, c, 16)
            act.wait_ge(mean_ready, 1)
            act.activation(small[:, 1], small[:, 0], ACT.Sqrt).then_inc(root_ready, 1)
            for n in range(EARLY):
                if n == EARLY - 1:
                    round_tile(0)
                act.wait_ge(mod_half_multiplied, n + 1)
                if n:
                    act.wait_ge(mod_in_bank, n)
                act.copy(mod_row[0:1, :], bank[6][0:1, :]).then_inc(mod_row_ready, 1)
            act.wait_ge(mod_ready, 1)
            for c in range(KC):
                act.activation(h_hi[:, c], x_rstd[:, c], ACT.Identity, scale=gain[:, 0, c:c + 1],
                               bias=mod[:, SHIFT_M + c:SHIFT_M + c + 1]).then_inc(h_hi_ready, 1)
                if c % 2 == 1 and c < KC - 1:
                    round_tile(c // 2 + 1)
            for t in range(T_VS, T_V):
                act.wait_ge(tile_done, t + 1)
                if t == T_V - 1:
                    for n in range(TT):
                        act.activation(vs[:, n], bank[n][:], ACT.Gelu_apprx_tanh).then_inc(vs_ready, 1)
                round_tile(t + SLOTS)
            for t in range(T_V, T_Q):
                act.wait_ge(tile_done, t + 1)
                round_tile(t + SLOTS)
            for n in range(TT):
                act.copy(v[:, n], bank[n][:]).then_inc(v_ready, 1)
            act.wait_ge(vs_mean_ready, 1)
            act.activation(small[:, 3], small[:, 2], ACT.Sqrt).then_inc(vs_root_ready, 1)
            for t in range(T_Q, T_U):
                act.wait_ge(tile_done, t + 1)
                c, scaled = (t - T_Q) % WC, t < T_K
                act.activation((qT if scaled else kT)[:, c], bank[4 + t % 2][:], ACT.Copy,
                               scale=HEAD_DIM ** -0.5 if scaled else 1.0).then_inc(proj_ready, 1)
                round_tile(t + SLOTS)
            for t in range(T_U, T_GATES):
                c = t - T_U
                act.wait_ge(tile_done, t + 1)
                if c >= 2:
                    act.wait_ge(gated, c - 1)
                act.activation(u[:, c % 2], bank[4 + t % 2][:], ACT.Gelu_apprx_tanh).then_inc(proj_ready, 1)
                round_tile(t + SLOTS)
                act.wait_ge(gated, c + 1)
                act.copy(sgu_hi[:, c], mix[:, c]).then_inc(sgu_hi_ready, 1)
            act.wait_ge(sgu_ready, WC)

            def stage_pair(p):
                act.copy(q_hi[:], qT[:, bass.ds(p, 1)].rearrange("p a t -> p (a t)")).then_inc(pair_hi, 1)
                act.copy(k_hi[:], kT[:, bass.ds(p, 1)].rearrange("p a t -> p (a t)")).then_inc(pair_hi, 1)

            def attend_pair(p, last):
                act.wait_ge(head_done, 2 * p + 1)
                act.copy(v_pair[:], v[:, :, bass.ds(p * P, P)]).then_inc(v_staged, 1)
                for i in range(11):
                    if i < 8:
                        act.wait_ge(scores_masked, 8 * p + i + 1 + 2)
                        width = (i % TT + 1) * P
                        act.activation(probs[:, i % 2, :width], probs[:, i % 2, :width], ACT.Exp, scale=-1.0,
                                       bias=small[:, 4, i % 2:i % 2 + 1],
                                       accum_out=small[:, 5, i % 2:i % 2 + 1]).then_inc(exp_done, 1)
                    if 2 <= i < 10:
                        n, qb = i - 2, (i - 2) % TT
                        act.wait_ge(probs_turned, 8 * p + n + 1 + 2)
                        if qb == 0:
                            act.wait_ge(head_done, 2 * p + n // TT + 1)
                        act.copy(probsT[:, :qb + 1, qb * P:(qb + 1) * P],
                                 bank[4 + n % 2][:, :(qb + 1) * P].rearrange("p (k q) -> p k q", q=P)) \
                            .then_inc(probsT_ready, 1)
                    if i == 8 and not last:
                        act.wait_ge(scores_done, 8 * p + 8)
                        stage_pair(p + 1)
                    if i in (2, 4, 7, 10):
                        j = (2, 4, 7, 10).index(i)
                        act.wait_ge(tile_done, T_GATES + 4 * p + j + 1)
                        act.activation(gates[:, bass.ds(4 * p + j, 1)].rearrange("p a t -> p (a t)"),
                                       bank[j % 2][:], ACT.Tanh, scale=0.5).then_inc(gate_ready, 1)
                        if j == 3:
                            act.wait_ge(head_done, 2 * p + 2 + 1)
                            act.copy(attn_hi[:, bass.ds(p, 1)].rearrange("p a t -> p (a t)"), bank[6][:]) \
                                .then_inc(attn_hi_ready, 1)
                        act.wait_ge(raw_landed[j], 16 * (p + T_GATES // SLOTS + 2))
                        act.copy(part_slot(w_hi, j), raw_slot(j)).then_inc(hi_ready, 1)

            stage_pair(0)
            with act.Fori(0, WC - 1) as p:
                attend_pair(p, False)
            attend_pair(WC - 1, True)

            with act.Fori(0, KC // SLOTS) as i:
                for s in range(SLOTS):
                    act.wait_ge(tile_done, T_BRANCH + SLOTS * i + s + 1)
                    act.wait_ge(raw_landed[s], 16 * (i + T_BRANCH // SLOTS + 2))
                    act.copy(part_slot(w_hi, s), raw_slot(s)).then_inc(hi_ready, 1)
                    act.wait_ge(merged, SLOTS * i + s + 1)
                    act.activation(h_hi[:, bass.ds(SLOTS * i + s, 1)].rearrange("p a t -> p (a t)"),
                                   work[:, s % 2], ACT.Copy, scale=0.5).then_inc(merged_hi, 1)
            with act.Fori(0, KC // SLOTS) as i:
                for s in range(SLOTS):
                    act.wait_ge(tile_done, T_OUT + SLOTS * i + s + 1)
                    act.wait_ge(raw_landed[s], 16 * (i + T_OUT // SLOTS + 2))
                    act.copy(part_slot(w_hi, s), raw_slot(s)).then_inc(hi_ready, 1)
                    act.wait_ge(mixed_in, SLOTS * i + s + 1 + 4)
                    act.wait_ge(square_added, KC + SLOTS * i + s + 1)
                    act.activation(squares[:, s % 2], x[:, bass.ds(SLOTS * i + s, 1)].rearrange("p a t -> p (a t)"),
                                   ACT.Square).then_inc(squared, 1)
            act.wait_ge(mean_ready, 2)
            act.activation(small[:, 1], small[:, 0], ACT.Sqrt).then_inc(root_ready, 1)
            for c in range(KC):
                act.wait_ge(normed, 2 * KC + c + 1)
                act.activation(h_hi[:, c], work[:, c % 2], ACT.Identity,
                               bias=mod[:, SHIFT_F + c:SHIFT_F + c + 1]).then_inc(h_hi_ready, 1)

            def mlp_pair(j, s, round_next):
                for half, conv in enumerate((conv_act, conv_lin)):
                    at = j + half * FC
                    act.wait_ge(tile_done, T_UP + 2 * j + half + 1)
                    act.activation(conv[:, s], bank[4 + 2 * s + half][:], ACT.Identity,
                                   scale=cols[:, bass.ds(at + C_WCONV + 2 * 2 * FC, 1)],
                                   bias=cols[:, bass.ds(at + C_BCONV, 1)]).then_inc(conv_begun, 1)
                    round_next(2 * s + half)
                    if half == 0:
                        act.wait_ge(conv_done, 2 * j + 1 + 4)
                        act.activation(conv_act[:, s], conv_act[:, s], ACT.Silu).then_inc(silu_done, 1)
                act.wait_ge(glu_ready, j + 1)
                act.copy(g_hi[:, bass.ds(j, 1)].rearrange("p a t -> p (a t)"), glu[:, s]).then_inc(g_hi_ready, 1)

            def round_down(n, landed):
                act.wait_ge(raw_landed[n % 2 * 2], landed)
                act.copy(down_slot(w_hi, n), down_slot(raw, n)).then_inc(hi_ready, 1)

            with act.Fori(0, FC // 2 - 1) as i:
                def round_next(s):
                    act.wait_ge(raw_landed[s], 16 * (i + T_UP // SLOTS + 2))
                    act.copy(part_slot(w_hi, s), raw_slot(s)).then_inc(hi_ready, 1)

                for s in range(2):
                    mlp_pair(2 * i + s, s, round_next)
            for s in range(2):
                mlp_pair(FC - 2 + s, s, lambda n: round_down(n // 2, 16 * (T_DOWN // SLOTS + 1)) if n % 2 else None)

            def down_chunk(c, s, round_next):
                for half in range(2):
                    act.wait_ge(tile_done, T_DOWN + 2 * c + half + 1)
                    if round_next:
                        round_down(half, 16 * (c + T_DOWN // SLOTS + 2))
                act.wait_ge(down_added, c + 1 + 2)
                act.wait_ge(square_added, 2 * KC + c + 1)
                act.activation(squares[:, s], x[:, bass.ds(c, 1)].rearrange("p a t -> p (a t)"), ACT.Square) \
                    .then_inc(squared, 1)

            with act.Fori(0, KC // 2 - 1) as i:
                for s in range(2):
                    down_chunk(2 * i + s, s, True)
            down_chunk(KC - 2, 0, True)
            down_chunk(KC - 1, 1, False)
            act.wait_ge(mean_ready, 3)
            act.activation(small[:, 1], small[:, 0], ACT.Sqrt).then_inc(root_ready, 1)

        @block.vector
        def _(dve):
            order = [0]

            def then(ins):
                order[0] += 1
                ins.then_inc(dve_order, 1)
                dve.wait_ge(dve_order, order[0])

            def add_square(slot, at):
                dve.wait_ge(squared, at)
                dve.tensor_tensor(sum_sq[:], sum_sq[:], squares[:, slot], ALU.add).then_inc(square_added, 1)
                dve.wait_ge(square_added, at + 2)

            def spread_rstd(n, stat_bank):
                dve.wait_ge(stats_done, n + 1)
                dve.tensor_scalar(small[:, 0], bank[stat_bank][:, 0:TT], 1.0 / D_MODEL, EPS, ALU.mult, ALU.add) \
                    .then_inc(mean_ready, 1)
                dve.wait_ge(root_ready, n + 1)
                then(dve.reciprocal(small[:, 6], small[:, 1]))
                if n:
                    dve.wait_ge(rstd_spread, TT * n)
                for t in range(TT):
                    dve.tensor_scalar(diag[:, t * P:(t + 1) * P], ident[:], small[:, 6, t:t + 1], None, ALU.mult) \
                        .then_inc(diag_ready, 1)

            def norm_chunks():
                dve.wait_ge(rstd_spread, 2 * TT)
                for c in range(KC + 1):
                    if c < KC:
                        dve.scalar_tensor_tensor(out=work[:, c % 2], in0=x[:, c], scalar=gain[:, 1, c:c + 1],
                                                 in1=bank[1][:], op0=ALU.mult, op1=ALU.mult) \
                            .then_inc(normed, 1)
                    if c:
                        dve.wait_ge(h_hi_ready, KC + c)
                        dve.scalar_tensor_tensor(out=h_lo[:, c - 1], in0=work[:, (c - 1) % 2],
                                                 scalar=mod[:, SHIFT_F + c - 1:SHIFT_F + c],
                                                 in1=h_hi[:, c - 1].bitcast(F32), op0=ALU.add, op1=ALU.subtract) \
                            .then_inc(h_ready, 1)
                        dve.wait_ge(h_ready, KC + c)

            def sum_mod_half(n, step):
                wait_mod_landed(dve, n)
                group = n // 2
                acc = mod_acc[:, group % ACCS]
                for r in range(4):
                    k = n % 2 * 4 + r
                    w = mod_half(n)[:, r]
                    if k == 0:
                        if group >= ACCS:
                            dve.wait_ge(mod_in_bank, group - ACCS + 1)
                        then(dve.tensor_scalar(acc, w, c_act[:, 0:1], None, ALU.mult))
                        continue
                    ins = dve.scalar_tensor_tensor(out=acc, in0=w, scalar=c_act[:, k:k + 1], in1=acc,
                                                   op0=ALU.mult, op1=ALU.add)
                    if r < 3:
                        then(ins)
                ins.then_inc(mod_half_summed, 1)
                dve.wait_ge(mod_half_summed, step + 1)

            dve.sem_inc(square_added, 2)
            dve.sem_inc(scores_masked, 2)
            dve.sem_inc(attn_ready, 1)
            dve.sem_inc(branch_read, 2)
            dve.sem_inc(mixed_in, 4)
            dve.sem_inc(conv_done, 4)
            dve.sem_inc(down_added, 2)
            then(dve.memset(sum_sq[:], 0.0))
            for c in range(KC):
                add_square(c % 2, c + 1)
            dve.wait_ge(consts_built, 2)
            spread_rstd(0, 4)
            dve.wait_ge(c_ready, 1)
            for n in range(EARLY):
                sum_mod_half(2 * n, n)
                if n == 0:
                    dve.wait_ge(rstd_spread, TT)
                for c in range(3 * n, min(3 * n + 3, KC)):
                    dve.tensor_tensor(x_rstd[:, c], x[:, c], bank[5][:], ALU.mult).then_inc(normed, 1)
            dve.wait_ge(mod_in_bank, EARLY)
            then(dve.tensor_tensor(mod[:, 0:2 * KC], bank[7][:, 0:2 * KC], cols[:, C_BMOD:C_BMOD + 2 * KC], ALU.add))
            dve.scalar_tensor_tensor(out=gain[:, 0], in0=mod[:, SCALE_M:SCALE_M + KC], scalar=1.0,
                                     in1=cols[:, C_GMIX:C_GMIX + KC], op0=ALU.add, op1=ALU.mult).then_inc(mod_ready, 1)
            dve.wait_ge(mod_ready, 1)
            dve.wait_ge(normed, KC)
            for c in range(KC + 1):
                if c < KC:
                    dve.tensor_scalar(work[:, c % 2], x_rstd[:, c], gain[:, 0, c:c + 1],
                                      mod[:, SHIFT_M + c:SHIFT_M + c + 1], ALU.mult, ALU.add).then_inc(normed, 1)
                if c:
                    dve.wait_ge(h_hi_ready, c)
                    dve.wait_ge(normed, KC + c)
                    dve.tensor_tensor(h_lo[:, c - 1], work[:, (c - 1) % 2], h_hi[:, c - 1].bitcast(F32),
                                      ALU.subtract).then_inc(h_ready, 1)
                    dve.wait_ge(h_ready, c)
            dve.memset(sum_sq[:], 0.0).then_inc(mod_ready, 1)

            def vs_mean_squares():
                for n in range(TT):
                    dve.wait_ge(vs_ready, n + 1)
                    then(dve.tensor_tensor_reduce(work[:, 0], vs[:, n], vs[:, n], 1.0, 0.0, ALU.mult, ALU.add,
                                                  small[:, 7, n:n + 1]))
                dve.tensor_scalar(small[:, 2], small[:, 7], 1.0 / WIDTH, EPS, ALU.mult, ALU.add) \
                    .then_inc(vs_mean_ready, 1)

            def vs_norm():
                dve.wait_ge(vs_root_ready, 1)
                then(dve.reciprocal(small[:, 2], small[:, 3]))
                dve.wait_ge(sgu_landed, 64)
                for n in range(TT):
                    dve.scalar_tensor_tensor(out=vs[:, n], in0=vs[:, n], scalar=small[:, 2, n:n + 1], in1=g_row[:],
                                             op0=ALU.mult, op1=ALU.mult).then_inc(vs_normed, 1)

            for group in range(EARLY, len(MOD_ORDER)):
                for n in (2 * group, 2 * group + 1):
                    sum_mod_half(n, n - EARLY)
                if group == 6:
                    vs_mean_squares()
                if group == 9:
                    vs_norm()
            dve.wait_ge(mod_in_bank, len(MOD_ORDER))
            then(dve.tensor_tensor(mod[:, 2 * KC:], bank[7][:, 2 * KC:6 * KC],
                                   cols[:, C_BMOD + 2 * KC:C_BMOD + 6 * KC], ALU.add))
            dve.scalar_tensor_tensor(out=gain[:, 1], in0=mod[:, SCALE_F:SCALE_F + KC], scalar=1.0,
                                     in1=cols[:, C_GFFN:C_GFFN + KC], op0=ALU.add, op1=ALU.mult).then_inc(mod_ready, 1)

            for c in range(WC):
                dve.wait_ge(spatial_done, c + 1)
                dve.tensor_tensor(mix[:, c].rearrange("p (n i) -> p n i", i=P),
                                  bank[c][:].rearrange("p (n i) -> p n i", i=P),
                                  b_row[:, c:c + 1].broadcast_to([P, TT, P]), ALU.add).then_inc(mix_ready, 1)
            dve.wait_ge(mix_ready, WC)
            for c in range(WC):
                dve.wait_ge(proj_ready, 2 * WC + c + 1)
                dve.tensor_tensor(mix[:, c], mix[:, c], u[:, c % 2], ALU.mult).then_inc(gated, 1)
                dve.wait_ge(sgu_hi_ready, c + 1)
                dve.tensor_tensor(sgu_lo[:, c], mix[:, c], sgu_hi[:, c].bitcast(F32), ALU.subtract) \
                    .then_inc(sgu_ready, 1)

            def stage_pair(p):
                dve.wait_ge(pair_hi, 2 * p + 1)
                dve.tensor_tensor(q_lo[:], qT[:, bass.ds(p, 1)].rearrange("p a t -> p (a t)"), q_hi[:].bitcast(F32),
                                  ALU.subtract).then_inc(pair_lo, 1)
                dve.wait_ge(pair_hi, 2 * p + 2)
                dve.tensor_tensor(k_lo[:], kT[:, bass.ds(p, 1)].rearrange("p a t -> p (a t)"), k_hi[:].bitcast(F32),
                                  ALU.subtract).then_inc(pair_lo, 1)

            def attend_pair(p, last):
                for i in range(9):
                    if i < 8:
                        width = (i % TT + 1) * P
                        dve.wait_ge(probs_turned, 8 * p + i + 1)
                        dve.wait_ge(scores_done, 8 * p + i + 1)
                        dve.sem_inc(scores_taken, 1)
                        dve.tensor_tensor_reduce(probs[:, i % 2, :width], bank[2 + i % 2][:, :width],
                                                 mask[:, SEQ - width:], -1.0, -MASKED,
                                                 ALU.add, ALU.min, small[:, 4, i % 2:i % 2 + 1]) \
                            .then_inc(scores_masked, 1)
                    if i:
                        n = i - 1
                        width = (n % TT + 1) * P
                        dve.wait_ge(exp_done, 8 * p + n + 1)
                        dve.reciprocal(small[:, 6, n % 2:n % 2 + 1], small[:, 5, n % 2:n % 2 + 1]) \
                            .then_inc(dve_order, 1)
                        dve.wait_ge(dve_order, 8 * p + order[0] + n + 1)
                        dve.tensor_scalar(probs[:, n % 2, :width], probs[:, n % 2, :width],
                                          small[:, 6, n % 2:n % 2 + 1], None, ALU.mult).then_inc(probs_ready, 1)
                if not last:
                    stage_pair(p + 1)
                dve.wait_ge(attn_hi_ready, p + 1)
                dve.tensor_tensor(attn_lo[:, bass.ds(p, 1)].rearrange("p a t -> p (a t)"), bank[6][:],
                                  attn_hi[:, bass.ds(p, 1)].rearrange("p a t -> p (a t)").bitcast(F32),
                                  ALU.subtract).then_inc(attn_ready, 1)

            stage_pair(0)
            with dve.Fori(0, WC - 1) as p:
                attend_pair(p, False)
            attend_pair(WC - 1, True)
            order[0] += 8 * WC

            with dve.Fori(0, KC // SLOTS) as i:
                for s in range(SLOTS):
                    b = s % 2 * 2
                    dve.wait_ge(tile_done, T_BRANCH + SLOTS * i + s + 1)
                    dve.scalar_tensor_tensor(out=work[:, s % 2],
                                             in0=gates[:, bass.ds(2 * SLOTS * i + 2 * s, 1)].rearrange("p a t -> p (a t)"),
                                             scalar=1.0, in1=bank[b][:], op0=ALU.add, op1=ALU.mult)
                    dve.scalar_tensor_tensor(out=squares[:, s % 2],
                                             in0=gates[:, bass.ds(2 * SLOTS * i + 2 * s + 1, 1)].rearrange("p a t -> p (a t)"),
                                             scalar=1.0, in1=bank[b + 1][:], op0=ALU.add, op1=ALU.mult) \
                        .then_inc(branch_read, 1)
                    dve.wait_ge(branch_read, SLOTS * i + s + 1 + 2)
                    dve.tensor_tensor(work[:, s % 2], work[:, s % 2], squares[:, s % 2], ALU.add).then_inc(merged, 1)
                    dve.wait_ge(merged_hi, SLOTS * i + s + 1)
                    dve.scalar_tensor_tensor(out=h_lo[:, bass.ds(SLOTS * i + s, 1)].rearrange("p a t -> p (a t)"),
                                             in0=work[:, s % 2], scalar=0.5,
                                             in1=h_hi[:, bass.ds(SLOTS * i + s, 1)].rearrange("p a t -> p (a t)").bitcast(F32),
                                             op0=ALU.mult, op1=ALU.subtract).then_inc(merged_ready, 1)
                    dve.wait_ge(merged_ready, SLOTS * i + s + 1)

            with dve.Fori(0, KC // SLOTS) as i:
                for s in range(SLOTS):
                    chunk = x[:, bass.ds(SLOTS * i + s, 1)].rearrange("p a t -> p (a t)")
                    dve.wait_ge(tile_done, T_OUT + SLOTS * i + s + 1)
                    dve.scalar_tensor_tensor(out=chunk, in0=bank[4 + s][:],
                                             scalar=mod[:, bass.ds(SLOTS * i + s + GATE_M, 1)], in1=chunk,
                                             op0=ALU.mult, op1=ALU.add).then_inc(mixed_in, 1)
                    add_square(s % 2, KC + SLOTS * i + s + 1)
            spread_rstd(1, 0)
            norm_chunks()
            dve.memset(sum_sq[:], 0.0).then_inc(mod_ready, 1)

            with dve.Fori(0, FC // 2) as i:
                for s in range(2):
                    j = 2 * i + s
                    for half, conv in enumerate((conv_act, conv_lin)):
                        product = bank[4 + 2 * s + half]
                        dve.wait_ge(conv_begun, 2 * j + half + 1)
                        dve.scalar_tensor_tensor(out=conv[:, s, 1:], in0=product[:, :SEQ - 1],
                                                 scalar=cols[:, bass.ds(j + (half * FC + C_WCONV + 2 * FC), 1)],
                                                 in1=conv[:, s, 1:], op0=ALU.mult, op1=ALU.add).then_inc(dve_order, 1)
                        dve.wait_ge(dve_order, 4 * i + (order[0] + 2 * s + half + 1))
                        dve.scalar_tensor_tensor(out=conv[:, s, 2:], in0=product[:, :SEQ - 2],
                                                 scalar=cols[:, bass.ds(j + (half * FC + C_WCONV), 1)],
                                                 in1=conv[:, s, 2:], op0=ALU.mult, op1=ALU.add).then_inc(conv_done, 1)
                    dve.wait_ge(silu_done, j + 1)
                    dve.wait_ge(conv_done, 2 * j + 2 + 4)
                    dve.tensor_tensor(glu[:, s], conv_act[:, s], conv_lin[:, s], ALU.mult).then_inc(glu_ready, 1)
                    dve.wait_ge(g_hi_ready, j + 1)
                    dve.tensor_tensor(g_lo[:, bass.ds(j, 1)].rearrange("p a t -> p (a t)"), glu[:, s],
                                      g_hi[:, bass.ds(j, 1)].rearrange("p a t -> p (a t)").bitcast(F32),
                                      ALU.subtract).then_inc(g_ready, 1)
                    dve.wait_ge(g_ready, j + 1)
            order[0] += 2 * FC

            with dve.Fori(0, KC // 2) as i:
                for s in range(2):
                    c = 2 * i + s
                    chunk = x[:, bass.ds(c, 1)].rearrange("p a t -> p (a t)")
                    dve.wait_ge(tile_done, T_DOWN + 2 * c + 2)
                    dve.scalar_tensor_tensor(out=chunk, in0=bank[s][:], scalar=mod[:, bass.ds(c + GATE_F, 1)], in1=chunk,
                                             op0=ALU.mult, op1=ALU.add).then_inc(down_added, 1)
                    add_square(s, 2 * KC + c + 1)
            spread_rstd(2, 2)
            dve.wait_ge(rstd_spread, 3 * TT)
            for c in range(KC):
                dve.scalar_tensor_tensor(out=x[:, c], in0=x[:, c], scalar=cols[:, C_GFIN + c:C_GFIN + c + 1],
                                         in1=bank[3][:], op0=ALU.mult, op1=ALU.mult).then_inc(out_ready, 1)

        @block.tensor
        def _(pe):
            def product(out_ap, left, right, left_cols, right_cols, first, last):
                passes = [(0, 0), (0, 1), (1, 0)]
                for n, (a, b) in enumerate(passes):
                    ins = pe.matmul(out_ap, left[a][left_cols], right[b][right_cols],
                                    start=first and n == 0, stop=last and n == 2)
                return ins

            w, h = (w_hi, w_lo), (h_hi, h_lo)

            def block_cols(slot, k):
                return (slice(None), slice(slot * TILE + k * P, slot * TILE + (k + 1) * P))

            def chunk(k):
                return (slice(None), k)

            def token_stats(n, stat_bank):
                pe.wait_ge(square_added, KC * (n + 1) + 2)
                for t in range(TT):
                    ins = pe.matmul(bank[stat_bank][:, t:t + 1], sum_sq[:, t * P:(t + 1) * P], ones[:, 0:1],
                                    start=True, stop=True)
                ins.then_inc(stats_done, 1)

            def spread(n, spread_bank):
                for t in range(TT):
                    pe.wait_ge(diag_ready, TT * n + t + 1)
                    pe.matmul(bank[spread_bank][:, t * P:(t + 1) * P], ones[:], diag[:, t * P:(t + 1) * P],
                              start=True, stop=True).then_inc(rstd_spread, 1)

            def mod_columns(group):
                if group < EARLY:
                    pe.wait_ge(mod_half_summed, group + 1)
                    pe.wait_ge(mod_row_ready, group + 1)
                else:
                    pe.wait_ge(mod_half_summed, 2 * group + 2 - EARLY)
                for m in range(4):
                    col = bank[7][:, MOD_ORDER[group] * 4 + m:MOD_ORDER[group] * 4 + m + 1]
                    ins = pe.matmul(col, mod_acc[:, group % ACCS, m * P:(m + 1) * P], ones[:, 0:1],
                                    start=True, stop=group >= EARLY)
                    if group < EARLY:
                        ins = pe.matmul(col, mod_row[0:1, m * P:(m + 1) * P], ones[0:1, 0:1], start=False, stop=True)
                ins.then_inc(mod_in_bank, 1)

            pe.sem_inc(probs_turned, 2)
            pe.sem_inc(head_done, 1)
            pe.wait_ge(consts_built, 2)
            token_stats(0, 4)
            spread(0, 5)
            pe.wait_ge(c_ready, 1)
            for group in range(EARLY):
                n = 2 * group + 1
                wait_mod_landed(pe, n)
                if group:
                    pe.wait_ge(mod_row_ready, group)
                for r in range(4):
                    ins = pe.matmul(bank[6][0:1, :], c_act[:, 4 + r:5 + r], mod_half(n)[:, r],
                                    start=r == 0, stop=r == 3)
                ins.then_inc(mod_half_multiplied, 1)
                mod_columns(group)

            for t in range(T_VS, T_Q):
                pe.wait_ge(lo_ready, t + 1)
                for kk in range(2):
                    k = t % 4 * 2 + kk
                    if t < T_V:
                        pe.wait_ge(h_ready, k + 1)
                    for n in range(TT):
                        if t == T_V and kk == 0:
                            pe.wait_ge(vs_ready, n + 1)
                        cols_w = (slice(None), slice(t % SLOTS * TILE + kk * 512, t % SLOTS * TILE + (kk + 1) * 512))
                        ins = product(bank[n][:], h, w, (slice(None), k, slice(n * P, (n + 1) * P)), cols_w,
                                      k == 0, k == KC - 1)
                ins.then_inc(tile_done, 1)
                if t % 2 and t > 1:
                    mod_columns(EARLY + t // 2 - 1)

            def project(t, target):
                for k in range(KC):
                    ins = product(target, w, h, block_cols(t % SLOTS, k), chunk(k), k == 0, k == KC - 1)
                ins.then_inc(tile_done, 1)

            for t in range(T_Q, T_GATES):
                pe.wait_ge(lo_ready, t + 1)
                if t >= T_Q + 2:
                    pe.wait_ge(proj_ready, t - T_Q - 1)
                elif t == T_Q:
                    pe.wait_ge(normed, KC)
                project(t, bank[4 + t % 2][:])
                if t % 2 and t < T_GATES - 2:
                    mod_columns(EARLY + t // 2 - 1)
                if t == T_U - 1:
                    pe.wait_ge(spatial_masked, 1)
                    pe.wait_ge(vs_normed, TT)
                    pe.wait_ge(v_ready, TT)
                    for c in range(WC):
                        for e in range(2):
                            g = 2 * c + e
                            for n in range(TT):
                                ins = pe.matmul(bank[c][64 * e:64 * e + 64, n * P:(n + 1) * P],
                                                vs[:, n, g * 64:(g + 1) * 64], w_spatial[:, g, :],
                                                start=True, stop=True)
                        ins.then_inc(spatial_done, 1)

            pe.wait_ge(mix_ready, WC)
            pe.wait_ge(proj_ready, 3 * WC)
            step_units = [4, 3, 3, 3, 3, 3, 3, 3, 3, 2, 2]
            with pe.Fori(0, WC) as p:
                unit = 0
                for i in range(11):
                    for _ in range(step_units[i]):
                        j, k = unit // UNITS, unit % UNITS
                        if k == 0:
                            pe.wait_ge(lo_ready, T_GATES + 4 * p + j + 1)
                            pe.wait_ge(gate_ready, 4 * p + j + 1)
                        ins = product(bank[j % 2][:], w, h, block_cols(j, k), chunk(k), k == 0, k == KC - 1)
                        if k == KC - 1:
                            ins.then_inc(tile_done, 1)
                        unit += 1
                    if i < 8:
                        e, qb = i // TT, i % TT
                        width = (qb + 1) * P
                        rows = slice(64 * e, 64 * e + 64)
                        if i == 0:
                            pe.wait_ge(pair_lo, 2 * p + 2)
                        pe.wait_ge(scores_masked, 8 * p + i + 1)
                        product(bank[2 + i % 2][:, :width], (q_hi, q_lo), (k_hi, k_lo),
                                (rows, slice(qb * P, width)), (rows, slice(0, width)), True, True) \
                            .then_inc(scores_done, 1)
                    if i in (6, 10):
                        e = (i - 6) // 4
                        pe.wait_ge(probsT_ready, 8 * p + 4 * e + 4 + 2)
                        if e == 0:
                            pe.wait_ge(v_staged, p + 1)
                            pe.wait_ge(attn_ready, p + 1)
                        for kb in range(TT):
                            ins = pe.matmul(bank[6][64 * e:64 * e + 64, kb * P:], v_pair[:, kb, 64 * e:64 * e + 64],
                                            probsT[:, kb, kb * P:], start=kb == 0, stop=kb == TT - 1)
                        ins.then_inc(head_done, 1)
                    if 2 <= i < 10:
                        n, qb = i - 2, (i - 2) % TT
                        pe.wait_ge(probs_ready, 8 * p + n + 1)
                        pe.wait_ge(probsT_ready, 8 * p + n + 1)
                        for kb in range(qb + 1):
                            ins = pe.transpose(bank[4 + n % 2][:, kb * P:(kb + 1) * P],
                                               probs[:, n % 2, kb * P:(kb + 1) * P], ident[:])
                        ins.then_inc(probs_turned, 1)

            pe.wait_ge(gate_ready, 2 * KC + 2)
            pe.wait_ge(sgu_ready, WC)
            with pe.Fori(0, KC // SLOTS) as i:
                for s in range(SLOTS):
                    pe.wait_ge(lo_ready, T_BRANCH + SLOTS * i + s + 1)
                    pe.wait_ge(branch_read, SLOTS * i + s + 1)
                    for k in [*range(WC, 2 * WC), *range(WC)]:
                        if s == 0 and k == 0:
                            pe.wait_ge(attn_ready, WC + 1)
                        branch = (attn_hi, attn_lo) if k < WC else (sgu_hi, sgu_lo)
                        ins = product(bank[s % 2 * 2 + k // WC][:], w, branch, block_cols(s, k), chunk(k % WC),
                                      k % WC == 0, k % WC == WC - 1)
                    ins.then_inc(tile_done, 1)

            pe.wait_ge(probsT_ready, 8 * WC + 2)
            pe.wait_ge(mod_ready, 3)
            with pe.Fori(0, KC // SLOTS) as i:
                for s in range(SLOTS):
                    pe.wait_ge(lo_ready, T_OUT + SLOTS * i + s + 1)
                    pe.wait_ge(mixed_in, SLOTS * i + s + 1)
                    for k in range(KC):
                        if s == 0:
                            pe.wait_ge(merged_ready, k + 1)
                        ins = product(bank[4 + s][:], w, h, block_cols(s, k), chunk(k), k == 0, k == KC - 1)
                    ins.then_inc(tile_done, 1)
            pe.wait_ge(branch_read, KC + 2)
            token_stats(1, 0)
            spread(1, 1)

            pe.wait_ge(mixed_in, KC + 4)
            pe.wait_ge(lo_ready, T_UP + 2)
            for k in range(KC):
                pe.wait_ge(h_ready, KC + k + 1)
                for s in range(2):
                    ins = product(bank[4 + s][:], w, h, block_cols(s, k), chunk(k), k == 0, k == KC - 1)
                    if k == KC - 1:
                        ins.then_inc(tile_done, 1)
            for s in range(2, SLOTS):
                pe.wait_ge(lo_ready, T_UP + s + 1)
                for k in range(KC):
                    ins = product(bank[4 + s][:], w, h, block_cols(s, k), chunk(k), k == 0, k == KC - 1)
                ins.then_inc(tile_done, 1)
            with pe.Fori(1, FC // 2) as i:
                for s in range(SLOTS):
                    pe.wait_ge(lo_ready, T_UP + SLOTS * i + s + 1)
                    pe.wait_ge(conv_done, SLOTS * i + s + 1)
                    for k in range(KC):
                        ins = product(bank[4 + s][:], w, h, block_cols(s, k), chunk(k), k == 0, k == KC - 1)
                    ins.then_inc(tile_done, 1)

            pe.wait_ge(g_ready, FC - 1)
            with pe.Fori(0, KC // 2) as i:
                for s in range(2):
                    pe.wait_ge(down_added, 2 * i + s + 1)
                    for half in range(2):
                        pe.wait_ge(lo_ready, T_DOWN + 4 * i + 2 * s + half + 1)
                        for r in range(DOWN_UNITS):
                            k = half * DOWN_UNITS + r
                            if k == FC - 1 and s == 0:
                                pe.wait_ge(g_ready, FC)
                            ins = product(bank[s][:], w, (g_hi, g_lo), block_cols(2 * half, r), chunk(k),
                                          k == 0, k == FC - 1)
                        ins.then_inc(tile_done, 1)
            token_stats(2, 2)
            spread(2, 3)


def kernel(**inputs):
    import numpy as np
    import concourse.bacc as bacc
    from concourse.bass_utils import run_bass_kernel_spmd

    def a(name):
        return np.asarray(inputs[name])

    def columns(v):
        return v.reshape(-1, P).T

    def by_columns(w):
        k, n = w.shape
        return w.reshape(k // P, P, n // P, P).transpose(2, 1, 0, 3).reshape(n // P, P, k)

    def by_rows(w):
        k, n = w.shape
        return w.reshape(k // (2 * P), 2, P, n).transpose(0, 2, 1, 3).reshape(k // (2 * P), P, 2 * n)

    def alternate(one, other):
        return np.stack([one, other], axis=1).reshape(-1, *one.shape[1:])

    w_in = a("w_in")[0]
    q, k, v, u, vs = (w_in[:, n * WIDTH:(n + 1) * WIDTH] for n in range(5))
    gate_a, gate_s = (w_in[:, 5 * WIDTH + n * D_MODEL:5 * WIDTH + (n + 1) * D_MODEL] for n in range(2))
    branches = np.concatenate([by_columns(a("w_attn_br")[0]), by_columns(a("w_sgu_br")[0])], axis=2)
    w_up = a("w_up")[0]
    tiles = np.concatenate([
        by_rows(vs), by_rows(v), by_columns(q), by_columns(k), by_columns(u),
        alternate(by_columns(gate_a), by_columns(gate_s)), branches, by_columns(a("w_out")[0]),
        alternate(by_columns(w_up[:, :D_FF]), by_columns(w_up[:, D_FF:]))])
    down = by_columns(a("w_down")[0]).reshape(KC, P, 2, DOWN_TILE).transpose(0, 2, 1, 3).reshape(N_DOWN, P, DOWN_TILE)
    arrays = {
        "xT": a("x")[0].T,
        "columns": np.concatenate([columns(a(n).reshape(-1)) for n in
                                   ("c", "b_mod", "g_mix", "g_ffn", "g_final", "w_conv", "b_conv")], axis=1),
        "w_mod": a("w_mod")[0],
        "tiles": tiles,
        "down_tiles": down,
        "w_sgu": a("w_sgu_s")[0].transpose(2, 0, 1),
        "g_sgu": a("g_sgu"),
        "b_sgu": a("b_sgu_s")[0],
    }
    arrays = {name: np.ascontiguousarray(v) for name, v in arrays.items()}
    nc = bacc.Bacc("TRN2", target_bir_lowering=False, num_devices=1, dynamic_dma_scratch_size=1024)
    aps = [nc.dram_tensor(name, v.shape, mybir.dt.from_np(v.dtype), kind="ExternalInput").ap()
           for name, v in arrays.items()]
    out = nc.dram_tensor("outT", (D_MODEL, SEQ), F32, kind="ExternalOutput").ap()
    decoder_layer(nc, *aps, out)
    r = run_bass_kernel_spmd(nc, [arrays], core_ids=[0])
    return np.ascontiguousarray(r.results[0]["outT"].T)[None]
```

```python
from contextlib import ExitStack

import concourse.bass as bass
from concourse import mybir

P = 128
D_MODEL, SEQ, HEADS, HEAD_DIM = 1024, 512, 8, 64
WIDTH = HEADS * HEAD_DIM
GROUPS = 8
D_FF = 2816
EPS = 1e-6
KC = D_MODEL // P
WC = WIDTH // P
FC = D_FF // P
TT = SEQ // P

T_Q, T_VS, T_V, T_K, T_U = 0, 4, 8, 12, 16
T_GATES = 20
T_BRANCH = T_GATES + 2 * KC
T_OUT = T_BRANCH + KC
T_UP = T_OUT + KC
T_DOWN = T_UP + 2 * FC
UNITS, DOWN_UNITS = 8, FC // 2
TILE, DOWN_TILE = UNITS * P, DOWN_UNITS * P
SLOTS = 4
N_DOWN = 2 * KC
POOL_OUT = (KC // 2 - 1, KC - 2)

C_C = 0
C_BMOD = C_C + KC
C_GMIX = C_BMOD + 6 * KC
C_GFFN = C_GMIX + KC
C_GFIN = C_GFFN + KC
C_WCONV = C_GFIN + KC
C_BCONV = C_WCONV + 3 * 2 * FC
N_COLS = C_BCONV + 2 * FC
SCALED = KC
SHIFT_M, SCALE_M, GATE_M, SHIFT_F, SCALE_F, GATE_F = (KC * n for n in range(6))
MOD_ORDER = [2, 3, 0, 1, 4, 5, 6, 7, 8, 9, 10, 11]
SHARED = 1
EARLY = 4
MOD_BUFS = 4
ACCS = 4
MOD_AFTER = [9, 10, 12, 13, 15, 16, 17, 18]
Q_BANKS = [4, 5, 0, 3]
V_BANKS = [4, 5, 6, 0]
UP_BANKS = [0, 3]

MASKED = -3.0e38
F32 = mybir.dt.float32
F32R = mybir.dt.float32r
BF16 = mybir.dt.bfloat16
ALU = mybir.AluOpType
ACT = mybir.ActivationFunctionType


def decoder_layer(nc, xT, cols_in, w_mod, tiles, down_tiles, w_sgu, g_sgu, b_sgu, out):
    with ExitStack() as ctx:
        def sem(name):
            return ctx.enter_context(nc.semaphore(name))

        def held(scope):
            return lambda name, shape, dt=F32: scope.enter_context(nc.sbuf_tensor(name, shape, dt))

        sb = held(ctx)
        x = sb("x", [P, KC, SEQ])
        h_hi = sb("h_hi", [P, KC, SEQ], F32R)
        h_lo = sb("h_lo", [P, KC, SEQ], F32R)
        raw = sb("raw", [P, SLOTS * TILE])
        w_hi = sb("w_hi", [P, SLOTS * TILE], F32R)
        w_lo = sb("w_lo", [P, SLOTS * TILE], F32R)
        cols = sb("cols", [P, N_COLS])
        c_act = sb("c_act", [P, KC])
        mod = sb("mod", [P, 6 * KC])
        gain = sb("gain", [P, 2, KC])
        shift_parts = sb("shift_parts", [P, 2, KC, 2], F32R)
        shifted = sb("shifted", [P, 2, WC])
        rstd = sb("rstd", [P, SEQ])
        small = sb("small", [P, 8, TT])
        ident = sb("ident", [P, P])
        ones = sb("ones", [P, P])
        mask = sb("mask", [P, SEQ], BF16)
        work = sb("work", [P, 2, SEQ])
        squares = sb("squares", [P, 2, SEQ])
        sum_sq = sb("sum_sq", [P, SEQ])
        diag = sum_sq
        probs = squares
        bank = [ctx.enter_context(nc.psum_tensor(f"bank{n}", [P, 512], F32)) for n in range(8)]

        with ExitStack() as mixing:
            sb = held(mixing)
            v = sb("v", [P, TT, WIDTH])
            qT = sb("qT", [P, WC, SEQ])
            kT = sb("kT", [P, WC, SEQ])
            with ExitStack() as early:
                sb = held(early)
                vs = sb("vs", [P, TT, WIDTH])
                mix = sb("mix", [P, WC, SEQ])
                u = sb("u", [P, 2, SEQ])
                w_spatial = sb("w_spatial", [P, GROUPS, P])
                g_row = sb("g_row", [P, WIDTH])
                b_row = sb("b_row", [P, WC, P])
                mod_w = sb("mod_w", [P, MOD_BUFS, 4, 512])
                mod_acc = sb("mod_acc", [P, ACCS, 512])
                mod_row = sb("mod_row", [P, 512])
            with ExitStack() as late:
                sb = held(late)
                gates = sb("gates", [P, 2 * KC, SEQ])
                attn_hi = sb("attn_hi", [P, WC, SEQ], F32R)
                attn_lo = sb("attn_lo", [P, WC, SEQ], F32R)
                sgu_hi = sb("sgu_hi", [P, WC, SEQ], F32R)
                sgu_lo = sb("sgu_lo", [P, WC, SEQ], F32R)
                q_parts = sb("q_parts", [P, 2, SEQ], F32R)
                k_lo = sb("k_lo", [P, SEQ], F32R)
                k_twice = sb("k_twice", [P, 2, SEQ], F32R)
                v_pair = sb("v_pair", [P, TT, P])
                probsT = sb("probsT", [P, TT, SEQ])
        with ExitStack() as mlp:
            sb = held(mlp)
            g_hi = sb("g_hi", [P, FC, SEQ], F32R)
            g_lo = sb("g_lo", [P, FC, SEQ], F32R)
            conv_act = sb("conv_act", [P, 2, SEQ])
            conv_lin = sb("conv_lin", [P, 2, SEQ])
            glu = sb("glu", [P, 2, SEQ])

        x_landed = [sem(f"x_landed{n}") for n in range(4)]
        cols_landed = sem("cols_landed")
        sgu_landed = sem("sgu_landed")
        mod_landed = [sem(f"mod_landed{n}") for n in range(2 * EARLY)]
        raw_landed = [sem(f"raw_landed{n}") for n in range(SLOTS)]
        out_landed = sem("out_landed")
        consts_built = sem("consts_built")
        pool_order = sem("pool_order")
        spatial_masked = sem("spatial_masked")
        hi_ready = sem("hi_ready")
        lo_ready = sem("lo_ready")
        tile_done = sem("tile_done")
        c_ready = sem("c_ready")
        mod_half_summed = sem("mod_half_summed")
        mod_half_multiplied = sem("mod_half_multiplied")
        mod_row_ready = sem("mod_row_ready")
        mod_summed = sem("mod_summed")
        mod_in_bank = sem("mod_in_bank")
        mod_ready = sem("mod_ready")
        squared = sem("squared")
        square_added = sem("square_added")
        stats_done = sem("stats_done")
        mean_ready = sem("mean_ready")
        root_ready = sem("root_ready")
        diag_ready = sem("diag_ready")
        rstd_spread = sem("rstd_spread")
        rstd_ready = sem("rstd_ready")
        scaled_hi = sem("scaled_hi")
        scaled_ready = sem("scaled_ready")
        scaled_used = sem("scaled_used")
        shift_ready = sem("shift_ready")
        first_done = sem("first_done")
        first_scaled = sem("first_scaled")
        shift_row_ready = sem("shift_row_ready")
        shift_in_bank = sem("shift_in_bank")
        shifted_ready = sem("shifted_ready")
        normed = sem("normed")
        h_hi_ready = sem("h_hi_ready")
        h_ready = sem("h_ready")
        vs_ready = sem("vs_ready")
        v_ready = sem("v_ready")
        proj_ready = sem("proj_ready")
        vs_mean_ready = sem("vs_mean_ready")
        vs_root_ready = sem("vs_root_ready")
        vs_normed = sem("vs_normed")
        spatial_done = sem("spatial_done")
        mix_ready = sem("mix_ready")
        gated = sem("gated")
        sgu_hi_ready = sem("sgu_hi_ready")
        sgu_ready = sem("sgu_ready")
        head_hi = sem("head_hi")
        head_staged = sem("head_staged")
        v_staged = sem("v_staged")
        scores_done = sem("scores_done")
        scores_masked = sem("scores_masked")
        scores_taken = sem("scores_taken")
        exp_done = sem("exp_done")
        probs_ready = sem("probs_ready")
        probs_turned = sem("probs_turned")
        probsT_ready = sem("probsT_ready")
        head_done = sem("head_done")
        attn_hi_ready = sem("attn_hi_ready")
        attn_ready = sem("attn_ready")
        gate_ready = sem("gate_ready")
        branch_read = sem("branch_read")
        merged = sem("merged")
        merged_hi = sem("merged_hi")
        merged_ready = sem("merged_ready")
        mixed_in = sem("mixed_in")
        pair_shifted = sem("pair_shifted")
        conv_begun = sem("conv_begun")
        conv_done = sem("conv_done")
        silu_done = sem("silu_done")
        glu_ready = sem("glu_ready")
        g_hi_ready = sem("g_hi_ready")
        g_ready = sem("g_ready")
        down_added = sem("down_added")
        dve_order = sem("dve_order")
        out_ready = sem("out_ready")
        pool_out_ready = sem("pool_out_ready")

        mod_view = w_mod.rearrange("(k p) n -> p k n", p=P)
        out_view = out.rearrange("(c p) t -> p c t", p=P)

        early_bufs = [mod_w[:, n] for n in range(MOD_BUFS)] + [v, qT, kT, mix]

        def mod_half(n):
            return early_bufs[n] if n < 2 * EARLY else mod_w[:, n % MOD_BUFS]

        def wait_mod_landed(engine, n):
            if n < 2 * EARLY:
                engine.wait_ge(mod_landed[n], 16)
            else:
                engine.wait_ge(mod_landed[n % MOD_BUFS], 16 * (n // MOD_BUFS))

        def raw_slot(tile):
            return raw[:, tile % SLOTS * TILE:(tile % SLOTS + 1) * TILE]

        def part_slot(part, slot):
            return part[:, slot * TILE:(slot + 1) * TILE]

        def down_slot(part, n):
            return part[:, n % 2 * 2 * TILE:n % 2 * 2 * TILE + DOWN_TILE]

        block = ctx.enter_context(nc.Block())

        @block.sync
        def _(sp):
            def load_mod_half(n):
                last = n - MOD_BUFS if n >= 2 * EARLY + MOD_BUFS else n - 2 * EARLY
                if last >= 2 * SHARED:
                    sp.wait_ge(mod_half_summed, last - SHARED + 1)
                elif last >= 0:
                    sp.wait_ge(mod_half_multiplied if last % 2 else mod_half_summed, last // 2 + 1)
                g, rows = MOD_ORDER[n // 2], n % 2 * 4
                sp.dma_start(mod_half(n)[:], mod_view[:, rows:rows + 4, g * 512:(g + 1) * 512]) \
                    .then_inc(mod_landed[n if n < 2 * EARLY else n % MOD_BUFS], 16)

            def load_tile(t):
                if t >= SLOTS:
                    sp.wait_ge(lo_ready, t - SLOTS + 1)
                sp.dma_start(raw_slot(t), tiles[t]).then_inc(raw_landed[t % SLOTS], 16)

            sp.dma_start(cols[:], cols_in).then_inc(cols_landed, 16)
            for n in range(EARLY):
                load_mod_half(n)
            load_tile(0)
            load_tile(1)
            for n in range(4):
                chunks = slice(n * KC // 4, (n + 1) * KC // 4)
                sp.dma_start(x[:, chunks], xT.rearrange("(c p) t -> p c t", p=P)[:, chunks]).then_inc(x_landed[n], 16)
            for n in range(EARLY, 2 * EARLY):
                load_mod_half(n)
                if n % 2:
                    load_tile(n // 2)
            for t in range(SLOTS, 2 * SLOTS):
                load_mod_half(t + SLOTS)
                load_tile(t)
            sp.dma_start(w_spatial[:], w_sgu).then_inc(sgu_landed, 16)
            sp.dma_start(g_row[:], bass.AP(tensor=g_sgu.tensor, offset=0, ap=[[0, P], [1, WIDTH]])) \
                .then_inc(sgu_landed, 16)
            for half in range(2):
                sp.dma_start(b_row[64 * half:64 * half + 64],
                             bass.AP(tensor=b_sgu.tensor, offset=half * P, ap=[[0, 64], [2 * P, WC], [1, P]])) \
                    .then_inc(sgu_landed, 16)
            for t in range(2 * SLOTS, 5 * SLOTS):
                load_tile(t)
                if t >= 5 * SLOTS - 6:
                    load_mod_half(2 * t - 4 * SLOTS)
                    load_mod_half(2 * t - 4 * SLOTS + 1)
            with sp.Fori(5, T_DOWN // SLOTS) as i:
                for s in range(SLOTS):
                    sp.wait_ge(lo_ready, SLOTS * i + s - SLOTS + 1)
                    sp.dma_start(raw_slot(s), tiles[bass.ds(SLOTS * i + s, 1)].rearrange("a p n -> p (a n)")) \
                        .then_inc(raw_landed[s], 16)
            for n in range(2):
                sp.wait_ge(lo_ready, T_DOWN - 2 + 2 * n)
                sp.dma_start(down_slot(raw, n), down_tiles[n]).then_inc(raw_landed[2 * n], 16)
            with sp.Fori(1, N_DOWN // 2) as i:
                for n in range(2):
                    sp.wait_ge(lo_ready, T_DOWN + 2 * i + n - 1)
                    sp.dma_start(down_slot(raw, n), down_tiles[bass.ds(2 * i + n, 1)].rearrange("a p n -> p (a n)")) \
                        .then_inc(raw_landed[2 * n], 16)
            for c in range(KC):
                pools = sum(n <= c for n in POOL_OUT)
                if c in POOL_OUT:
                    sp.wait_ge(pool_out_ready, pools)
                else:
                    sp.wait_ge(out_ready, c + 1 - pools)
                sp.dma_start(out_view[:, c], x[:, c]).then_inc(out_landed, 16)
            sp.wait_ge(out_landed, 16 * KC)

        @block.gpsimd
        def _(pool):
            pool.memset(ones[:], 1.0).then_inc(pool_order, 1)
            pool.memset(mask[:], 0.0).then_inc(pool_order, 1)
            pool.memset(sum_sq[:], 0.0).then_inc(pool_order, 1)
            pool.wait_ge(pool_order, 2)
            pool.affine_select(out=ident[:], in_=ones[:], compare_op=ALU.is_equal, fill=0.0, base=0,
                               pattern=[[-1, P]], channel_multiplier=1).then_inc(consts_built, 1)
            pool.affine_select(out=mask[:], in_=mask[:], compare_op=ALU.is_ge, fill=MASKED, base=3 * P,
                               pattern=[[-1, SEQ]], channel_multiplier=1).then_inc(consts_built, 1)
            def split_tiles(i, slots=range(SLOTS)):
                for s in slots:
                    pool.wait_ge(hi_ready, SLOTS * i + s + 1)
                    pool.tensor_tensor(part_slot(w_lo, s), raw_slot(s), part_slot(w_hi, s).bitcast(F32),
                                       ALU.subtract).then_inc(lo_ready, 1)

            split_tiles(0, (0, 1))
            pool.wait_ge(pool_order, 3)
            for c in range(KC):
                pool.wait_ge(squared, c + 1)
                pool.tensor_tensor(sum_sq[:], sum_sq[:], squares[:, c % 2], ALU.add).then_inc(square_added, 1)
                pool.wait_ge(square_added, c + 1 + 2)
            split_tiles(0, (2, 3))
            split_tiles(1)
            pool.wait_ge(sgu_landed, 64)
            pool.affine_select(out=w_spatial[:], in_=w_spatial[:], compare_op=ALU.is_ge, fill=0.0, base=0,
                               pattern=[[0, GROUPS], [1, P]], channel_multiplier=-1).then_inc(spatial_masked, 1)
            with pool.Fori(2, T_DOWN // SLOTS) as i:
                split_tiles(i)
            with pool.Fori(0, N_DOWN // 2) as i:
                for n in range(2):
                    pool.wait_ge(hi_ready, T_DOWN + 2 * i + n + 1)
                    pool.tensor_tensor(down_slot(w_lo, n), down_slot(raw, n), down_slot(w_hi, n).bitcast(F32),
                                       ALU.subtract).then_inc(lo_ready, 1)
            pool.wait_ge(rstd_ready, 3)
            for n, c in enumerate(POOL_OUT):
                pool.wait_ge(scaled_hi, 2 * KC + n + 1)
                pool.tensor_tensor(x[:, c], x[:, c], rstd[:], ALU.mult).then_inc(pool_out_ready, 1)

        @block.scalar
        def _(act):
            def round_tile(t):
                s = t % SLOTS
                act.wait_ge(raw_landed[s], 16 * (t // SLOTS + 1))
                act.copy(part_slot(w_hi, s), raw_slot(s)).then_inc(hi_ready, 1)

            act.sem_inc(probsT_ready, 2)
            act.sem_inc(gate_ready, 2)
            act.wait_ge(cols_landed, 16)
            act.activation(c_act[:], cols[:, C_C:C_C + KC], ACT.Silu).then_inc(c_ready, 1)
            act.wait_ge(mod_half_multiplied, 1)
            act.copy(mod_row[0:1, :], bank[6][0:1, :]).then_inc(mod_row_ready, 1)
            round_tile(0)
            round_tile(1)
            act.wait_ge(mod_ready, 1)
            for c in range(KC):
                act.wait_ge(x_landed[c // (KC // 4)], 16)
                act.activation(h_hi[:, c], x[:, c], ACT.Copy, scale=gain[:, 0, c:c + 1]).then_inc(scaled_hi, 1)
                act.wait_ge(square_added, c + 1)
                act.activation(squares[:, c % 2], x[:, c], ACT.Square).then_inc(squared, 1)
            round_tile(2)
            round_tile(3)
            act.wait_ge(mean_ready, 1)
            act.activation(small[:, 1], small[:, 0], ACT.Sqrt).then_inc(root_ready, 1)
            act.wait_ge(rstd_spread, TT)
            act.copy(rstd[:], bank[1][:]).then_inc(rstd_ready, 1)

            def norm_hi(n, shift, between):
                for c in range(KC):
                    between(c)
                    act.wait_ge(normed, n * KC + c + 1)
                    if n == 0 and c < KC - 1:
                        act.wait_ge(scaled_used, c + 1)
                    elif n == 0:
                        act.wait_ge(tile_done, T_VS)
                    act.activation(h_hi[:, c], work[:, c % 2], ACT.Identity,
                                   bias=mod[:, shift + c:shift + c + 1]).then_inc(h_hi_ready, 1)

            def round_next_of_q(c):
                if c % 2 == 0:
                    act.wait_ge(tile_done, T_Q + c // 2 + 1)
                    round_tile(T_Q + c // 2 + SLOTS)
                if c == 3:
                    act.copy(mod_row[0:2, :], bank[6][0:2, :]).then_inc(shift_row_ready, 1)

            norm_hi(0, SHIFT_M, round_next_of_q)
            act.wait_ge(shifted_ready, 1)
            for c in range(WC):
                act.activation(qT[:, c], qT[:, c], ACT.Identity, scale=HEAD_DIM ** -0.5,
                               bias=shifted[:, 0, c:c + 1]).then_inc(proj_ready, 1)
            for t in range(T_VS, T_V):
                act.wait_ge(tile_done, t + 1)
                if t == T_V - 1:
                    for n in range(TT):
                        act.activation(vs[:, n], bank[n][:], ACT.Gelu_apprx_tanh).then_inc(vs_ready, 1)
                round_tile(t + SLOTS)
            for t in range(T_V, T_K):
                act.wait_ge(tile_done, t + 1)
                round_tile(t + SLOTS)
                if t == T_V + 1:
                    act.wait_ge(vs_mean_ready, 1)
                    act.activation(small[:, 3], small[:, 2], ACT.Sqrt).then_inc(vs_root_ready, 1)
            for n in range(TT):
                act.copy(v[:, n], bank[V_BANKS[n]][:]).then_inc(v_ready, 1)
            for t in range(T_K, T_U):
                act.wait_ge(tile_done, t + 1)
                act.copy(kT[:, t - T_K], bank[1 + t % 2][:]).then_inc(proj_ready, 1)
                round_tile(t + SLOTS)
            def stage_head(p, e):
                own = slice(64 * e, 64 * e + 64)
                act.copy(q_parts[own, e], qT[own, bass.ds(p, 1)].rearrange("p a t -> p (a t)")).then_inc(head_hi, 1)
                act.copy(k_twice[own, e], kT[own, bass.ds(p, 1)].rearrange("p a t -> p (a t)")).then_inc(head_hi, 1)

            for t in range(T_U, T_GATES):
                c = t - T_U
                if t == T_GATES - 1:
                    act.wait_ge(mod_in_bank, len(MOD_ORDER))
                    for e in range(2):
                        stage_head(0, e)
                act.wait_ge(tile_done, t + 1)
                if c >= 2:
                    act.wait_ge(gated, c - 1)
                act.activation(u[:, c % 2], bank[4 + t % 2][:], ACT.Gelu_apprx_tanh).then_inc(proj_ready, 1)
                round_tile(t + SLOTS)
                act.wait_ge(gated, c + 1)
                act.copy(sgu_hi[:, c], mix[:, c]).then_inc(sgu_hi_ready, 1)
            act.wait_ge(sgu_ready, WC)

            def attend_pair(p, last):
                act.wait_ge(head_done, 2 * p + 1)
                act.copy(v_pair[:], v[:, :, bass.ds(p * P, P)]).then_inc(v_staged, 1)
                for i in range(11):
                    if i < 8:
                        act.wait_ge(scores_masked, 8 * p + i + 1 + 2)
                        width = (i % TT + 1) * P
                        act.activation(probs[:, i % 2, :width], probs[:, i % 2, :width], ACT.Exp, scale=-1.0,
                                       bias=small[:, 4, i % 2:i % 2 + 1],
                                       accum_out=small[:, 5, i % 2:i % 2 + 1]).then_inc(exp_done, 1)
                    if 2 <= i < 10:
                        n, qb = i - 2, (i - 2) % TT
                        act.wait_ge(probs_turned, 8 * p + n + 1 + 2)
                        if qb == 0:
                            act.wait_ge(head_done, 2 * p + n // TT + 1)
                        act.copy(probsT[:, :qb + 1, qb * P:(qb + 1) * P],
                                 bank[4 + n % 2][:, :(qb + 1) * P].rearrange("p (k q) -> p k q", q=P)) \
                            .then_inc(probsT_ready, 1)
                    if i == 8 and not last:
                        act.wait_ge(scores_done, 8 * p + 8)
                        stage_head(p + 1, 0)
                    if i in (2, 4, 7, 10):
                        j = (2, 4, 7, 10).index(i)
                        act.wait_ge(tile_done, T_GATES + 4 * p + j + 1)
                        act.activation(gates[:, bass.ds(4 * p + j, 1)].rearrange("p a t -> p (a t)"),
                                       bank[j % 2][:], ACT.Tanh, scale=0.5).then_inc(gate_ready, 1)
                        if j == 3:
                            act.wait_ge(head_done, 2 * p + 2 + 1)
                            act.copy(attn_hi[:, bass.ds(p, 1)].rearrange("p a t -> p (a t)"), bank[6][:]) \
                                .then_inc(attn_hi_ready, 1)
                        act.wait_ge(raw_landed[j], 16 * (p + T_GATES // SLOTS + 2))
                        act.copy(part_slot(w_hi, j), raw_slot(j)).then_inc(hi_ready, 1)
                if not last:
                    stage_head(p + 1, 1)

            with act.Fori(0, WC - 1) as p:
                attend_pair(p, False)
            attend_pair(WC - 1, True)

            with act.Fori(0, KC // SLOTS) as i:
                for s in range(SLOTS):
                    act.wait_ge(tile_done, T_BRANCH + SLOTS * i + s + 1)
                    act.wait_ge(raw_landed[s], 16 * (i + T_BRANCH // SLOTS + 2))
                    act.copy(part_slot(w_hi, s), raw_slot(s)).then_inc(hi_ready, 1)
                    act.wait_ge(merged, SLOTS * i + s + 1)
                    act.activation(h_hi[:, bass.ds(SLOTS * i + s, 1)].rearrange("p a t -> p (a t)"),
                                   work[:, s % 2], ACT.Copy, scale=0.5).then_inc(merged_hi, 1)
            act.wait_ge(mod_ready, 3)
            with act.Fori(0, KC // SLOTS) as i:
                for s in range(SLOTS):
                    act.wait_ge(tile_done, T_OUT + SLOTS * i + s + 1)
                    act.wait_ge(raw_landed[s], 16 * (i + T_OUT // SLOTS + 2))
                    act.copy(part_slot(w_hi, s), raw_slot(s)).then_inc(hi_ready, 1)
                    act.wait_ge(mixed_in, SLOTS * i + s + 1 + 4)
                    act.wait_ge(square_added, KC + SLOTS * i + s + 1)
                    act.activation(squares[:, s % 2], x[:, bass.ds(SLOTS * i + s, 1)].rearrange("p a t -> p (a t)"),
                                   ACT.Square).then_inc(squared, 1)
                    act.activation(g_hi[:, bass.ds(SLOTS * i + s + SCALED, 1)].rearrange("p a t -> p (a t)"),
                                   x[:, bass.ds(SLOTS * i + s, 1)].rearrange("p a t -> p (a t)"), ACT.Copy,
                                   scale=gain[:, 1, bass.ds(SLOTS * i + s, 1)]).then_inc(scaled_hi, 1)
            act.wait_ge(mean_ready, 2)
            act.activation(small[:, 1], small[:, 0], ACT.Sqrt).then_inc(root_ready, 1)
            act.wait_ge(rstd_spread, 2 * TT)
            act.copy(rstd[:], bank[1][:]).then_inc(rstd_ready, 1)

            def round_next_of_up(c):
                if c == 3:
                    act.wait_ge(tile_done, T_UP + 2)
                    act.copy(glu[0:2, 0, :2 * P], bank[2][0:2, :2 * P]).then_inc(shift_row_ready, 1)
                    round_tile(T_UP + SLOTS)
                    round_tile(T_UP + SLOTS + 1)

            norm_hi(1, SHIFT_F, round_next_of_up)

            def mlp_pair(j, s, round_next, products=None):
                for half, conv in enumerate((conv_act, conv_lin)):
                    at = j + half * FC
                    act.wait_ge(tile_done, T_UP + 2 * j + half + 1)
                    product = bank[4 + 2 * s + half][:] if products is None else products[:, half]
                    act.activation(conv[:, s], product, ACT.Identity,
                                   scale=cols[:, bass.ds(at + C_WCONV + 2 * 2 * FC, 1)],
                                   bias=cols[:, bass.ds(at + C_BCONV, 1)]).then_inc(conv_begun, 1)
                    round_next(2 * s + half)
                    if half == 0:
                        act.wait_ge(conv_done, 2 * j + 1 + 4)
                        act.activation(conv_act[:, s], conv_act[:, s], ACT.Silu).then_inc(silu_done, 1)
                act.wait_ge(glu_ready, j + 1)
                act.copy(g_hi[:, bass.ds(j, 1)].rearrange("p a t -> p (a t)"), glu[:, s]).then_inc(g_hi_ready, 1)

            def round_down(n, landed):
                act.wait_ge(raw_landed[n % 2 * 2], landed)
                act.copy(down_slot(w_hi, n), down_slot(raw, n)).then_inc(hi_ready, 1)

            def mlp_pairs(i, first):
                def round_next(s):
                    act.wait_ge(raw_landed[s], 16 * (i + T_UP // SLOTS + 2))
                    act.copy(part_slot(w_hi, s), raw_slot(s)).then_inc(hi_ready, 1)

                for s in range(2):
                    if first and s == 0:
                        act.wait_ge(shifted_ready, 2)
                        for half in range(2):
                            act.wait_ge(first_scaled, WC + half + 1)
                            act.activation(squares[:, half], squares[:, half], ACT.Identity,
                                           bias=shifted[:, 1, half:half + 1]).then_inc(pair_shifted, 1)
                        act.wait_ge(pair_shifted, 2)
                        act.wait_ge(tile_done, T_UP + SLOTS)
                        mlp_pair(0, 0, lambda n: round_next(n + 2), squares)
                    else:
                        mlp_pair(2 * i + s, s, (lambda n: None) if first else round_next)

            mlp_pairs(0, True)
            with act.Fori(1, FC // 2 - 1) as i:
                mlp_pairs(i, False)
            for s in range(2):
                mlp_pair(FC - 2 + s, s, lambda n: round_down(n // 2, 16 * (T_DOWN // SLOTS + 1)) if n % 2 else None)

            def down_chunk(c, s, round_next):
                for half in range(2):
                    act.wait_ge(tile_done, T_DOWN + 2 * c + half + 1)
                    if round_next:
                        round_down(half, 16 * (c + T_DOWN // SLOTS + 2))
                act.wait_ge(down_added, c + 1 + 2)
                act.wait_ge(square_added, 2 * KC + c + 1)
                act.activation(squares[:, s], x[:, bass.ds(c, 1)].rearrange("p a t -> p (a t)"), ACT.Square) \
                    .then_inc(squared, 1)

            with act.Fori(0, KC // 2 - 1) as i:
                for s in range(2):
                    down_chunk(2 * i + s, s, True)
            down_chunk(KC - 2, 0, True)
            act.wait_ge(squared, 3 * KC - 1)
            for c in POOL_OUT:
                act.activation(x[:, c], x[:, c], ACT.Copy, scale=cols[:, C_GFIN + c:C_GFIN + c + 1]) \
                    .then_inc(scaled_hi, 1)
            down_chunk(KC - 1, 1, False)
            act.wait_ge(mean_ready, 3)
            act.activation(small[:, 1], small[:, 0], ACT.Sqrt).then_inc(root_ready, 1)
            act.wait_ge(rstd_spread, 3 * TT)
            act.copy(rstd[:], bank[3][:]).then_inc(rstd_ready, 1)

        @block.vector
        def _(dve):
            order = [0]

            def then(ins):
                order[0] += 1
                ins.then_inc(dve_order, 1)
                dve.wait_ge(dve_order, order[0])

            def add_square(slot, at):
                dve.wait_ge(squared, at)
                dve.tensor_tensor(sum_sq[:], sum_sq[:], squares[:, slot], ALU.add).then_inc(square_added, 1)
                dve.wait_ge(square_added, at + 2)

            def spread_rstd(n, stat_bank):
                dve.wait_ge(stats_done, n + 1)
                sums = bank[stat_bank][:, 0:TT]
                if n == 2:
                    sums = small[:, 0]
                    then(dve.tensor_reduce(sums, bank[stat_bank][:, 0:2 * TT].rearrange("p (t n) -> p t n", n=2),
                                           mybir.AxisListType.X, ALU.add))
                dve.tensor_scalar(small[:, 0], sums, 1.0 / D_MODEL, EPS, ALU.mult, ALU.add) \
                    .then_inc(mean_ready, 1)
                dve.wait_ge(root_ready, n + 1)
                then(dve.reciprocal(small[:, 6], small[:, 1]))
                if n:
                    dve.wait_ge(rstd_spread, TT * n)
                for t in range(TT):
                    dve.tensor_scalar(diag[:, t * P:(t + 1) * P], ident[:], small[:, 6, t:t + 1], None, ALU.mult) \
                        .then_inc(diag_ready, 1)

            def norm_chunks(n, shift, between=None):
                dve.wait_ge(rstd_ready, n + 1)
                for c in range(KC + 1):
                    if c < KC:
                        dve.scalar_tensor_tensor(out=work[:, c % 2], in0=x[:, c], scalar=gain[:, n, c:c + 1],
                                                 in1=rstd[:], op0=ALU.mult, op1=ALU.mult) \
                            .then_inc(normed, 1)
                    if c:
                        dve.wait_ge(h_hi_ready, n * KC + c)
                        dve.scalar_tensor_tensor(out=h_lo[:, c - 1], in0=work[:, (c - 1) % 2],
                                                 scalar=mod[:, shift + c - 1:shift + c],
                                                 in1=h_hi[:, c - 1].bitcast(F32), op0=ALU.add, op1=ALU.subtract) \
                            .then_inc(h_ready, 1)
                        dve.wait_ge(h_ready, n * KC + c)
                    if c == 2 and between:
                        between()

            def split_shift(n, shift):
                then(dve.tensor_copy(shift_parts[:, n, :, 0], mod[:, shift:shift + KC]))
                dve.tensor_tensor(shift_parts[:, n, :, 1], mod[:, shift:shift + KC],
                                  shift_parts[:, n, :, 0].bitcast(F32), ALU.subtract).then_inc(shift_ready, 1)

            def sum_mod_half(n):
                wait_mod_landed(dve, n)
                group = n // 2
                acc = mod_acc[:, group % ACCS]
                for r in range(4):
                    k = n % 2 * 4 + r
                    w = mod_half(n)[:, r]
                    if k == 0:
                        if group >= ACCS:
                            dve.wait_ge(mod_in_bank, group - ACCS + 1)
                        then(dve.tensor_scalar(acc, w, c_act[:, 0:1], None, ALU.mult))
                        continue
                    ins = dve.scalar_tensor_tensor(out=acc, in0=w, scalar=c_act[:, k:k + 1], in1=acc,
                                                   op0=ALU.mult, op1=ALU.add)
                    if r < 3:
                        then(ins)
                ins.then_inc(mod_half_summed, 1)
                dve.wait_ge(mod_half_summed, n // 2 + 1 if n < 2 * SHARED else n - SHARED + 1)

            dve.sem_inc(square_added, 2)
            dve.sem_inc(scores_masked, 2)
            dve.sem_inc(attn_ready, 1)
            dve.sem_inc(branch_read, 2)
            dve.sem_inc(mixed_in, 4)
            dve.sem_inc(conv_done, 4)
            dve.sem_inc(down_added, 2)
            dve.wait_ge(c_ready, 1)
            for n in (0, 2, 3):
                sum_mod_half(n)
            dve.wait_ge(mod_in_bank, EARLY // 2)
            then(dve.tensor_tensor(mod[:, SCALE_M:SCALE_M + KC], bank[7][:, SCALE_M:SCALE_M + KC],
                                   cols[:, C_BMOD + SCALE_M:C_BMOD + SCALE_M + KC], ALU.add))
            dve.scalar_tensor_tensor(out=gain[:, 0], in0=mod[:, SCALE_M:SCALE_M + KC], scalar=1.0,
                                     in1=cols[:, C_GMIX:C_GMIX + KC], op0=ALU.add, op1=ALU.mult).then_inc(mod_ready, 1)
            dve.wait_ge(mod_ready, 1)
            for c in range(KC):
                dve.wait_ge(scaled_hi, c + 1)
                dve.scalar_tensor_tensor(out=h_lo[:, c], in0=x[:, c], scalar=gain[:, 0, c:c + 1],
                                         in1=h_hi[:, c].bitcast(F32), op0=ALU.mult, op1=ALU.subtract) \
                    .then_inc(scaled_ready, 1)

            def first_over_rms(n, source, to):
                if n == WC - 1:
                    dve.wait_ge(tile_done, T_VS)
                else:
                    dve.wait_ge(first_done, n + 1 - (n >= WC))
                dve.tensor_tensor(to, source[:], rstd[:], ALU.mult).then_inc(first_scaled, 1)

            for n in range(EARLY, 2 * EARLY):
                sum_mod_half(n)
            dve.wait_ge(consts_built, 2)
            spread_rstd(0, 2)
            dve.wait_ge(mod_in_bank, EARLY)
            then(dve.tensor_tensor(mod[:, SHIFT_M:SHIFT_M + KC], bank[7][:, SHIFT_M:SHIFT_M + KC],
                                   cols[:, C_BMOD + SHIFT_M:C_BMOD + SHIFT_M + KC], ALU.add))
            split_shift(0, SHIFT_M)
            dve.wait_ge(rstd_ready, 1)
            for c in range(WC - 1):
                first_over_rms(c, bank[Q_BANKS[c]], qT[:, c])
            norm_chunks(0, SHIFT_M, lambda: first_over_rms(3, bank[Q_BANKS[3]], qT[:, 3]))
            dve.wait_ge(shift_in_bank, 1)
            dve.tensor_scalar(shifted[:, 0], bank[6][:, 0:WC], HEAD_DIM ** -0.5, None, ALU.mult) \
                .then_inc(shifted_ready, 1)
            dve.memset(sum_sq[:], 0.0).then_inc(mod_ready, 1)

            def vs_mean_squares():
                for n in range(TT):
                    dve.wait_ge(vs_ready, n + 1)
                    then(dve.tensor_tensor_reduce(work[:, 0], vs[:, n], vs[:, n], 1.0, 0.0, ALU.mult, ALU.add,
                                                  small[:, 7, n:n + 1]))
                dve.tensor_scalar(small[:, 2], small[:, 7], 1.0 / WIDTH, EPS, ALU.mult, ALU.add) \
                    .then_inc(vs_mean_ready, 1)

            def vs_norm():
                dve.wait_ge(vs_root_ready, 1)
                then(dve.reciprocal(small[:, 2], small[:, 3]))
                dve.wait_ge(sgu_landed, 64)
                for n in range(TT):
                    dve.scalar_tensor_tensor(out=vs[:, n], in0=vs[:, n], scalar=small[:, 2, n:n + 1], in1=g_row[:],
                                             op0=ALU.mult, op1=ALU.mult).then_inc(vs_normed, 1)

            for group in range(EARLY, len(MOD_ORDER)):
                for n in (2 * group, 2 * group + 1):
                    sum_mod_half(n)
                if group == 5:
                    vs_mean_squares()
                if group == 8:
                    vs_norm()
            for c in range(WC):
                dve.wait_ge(spatial_done, c + 1)
                dve.tensor_tensor(mix[:, c].rearrange("p (n i) -> p n i", i=P),
                                  bank[c][:].rearrange("p (n i) -> p n i", i=P),
                                  b_row[:, c:c + 1].broadcast_to([P, TT, P]), ALU.add).then_inc(mix_ready, 1)
            dve.wait_ge(mix_ready, WC)
            def stage_head(p, e):
                own, other = slice(64 * e, 64 * e + 64), slice(64 - 64 * e, 128 - 64 * e)
                dve.wait_ge(head_hi, 4 * p + 2 * e + 1)
                dve.tensor_tensor(q_parts[other, e], qT[own, bass.ds(p, 1)].rearrange("p a t -> p (a t)"),
                                  q_parts[own, e].bitcast(F32), ALU.subtract).then_inc(head_staged, 1)
                dve.wait_ge(head_hi, 4 * p + 2 * e + 2)
                dve.tensor_copy(k_twice[other, e], k_twice[own, e]).then_inc(head_staged, 1)
                dve.tensor_tensor(k_lo[own], kT[own, bass.ds(p, 1)].rearrange("p a t -> p (a t)"),
                                  k_twice[own, e].bitcast(F32), ALU.subtract).then_inc(head_staged, 1)

            for c in range(WC):
                if c == WC - 1:
                    for e in range(2):
                        stage_head(0, e)
                dve.wait_ge(proj_ready, 2 * WC + c + 1)
                dve.tensor_tensor(mix[:, c], mix[:, c], u[:, c % 2], ALU.mult).then_inc(gated, 1)
                dve.wait_ge(sgu_hi_ready, c + 1)
                dve.tensor_tensor(sgu_lo[:, c], mix[:, c], sgu_hi[:, c].bitcast(F32), ALU.subtract) \
                    .then_inc(sgu_ready, 1)

            dve.wait_ge(mod_in_bank, len(MOD_ORDER))
            then(dve.tensor_tensor(mod[:, 2 * KC:], bank[7][:, 2 * KC:6 * KC],
                                   cols[:, C_BMOD + 2 * KC:C_BMOD + 6 * KC], ALU.add))
            dve.scalar_tensor_tensor(out=gain[:, 1], in0=mod[:, SCALE_F:SCALE_F + KC], scalar=1.0,
                                     in1=cols[:, C_GFFN:C_GFFN + KC], op0=ALU.add, op1=ALU.mult).then_inc(mod_ready, 1)
            split_shift(1, SHIFT_F)

            def attend_pair(p, last):
                for i in range(9):
                    if i < 8:
                        width = (i % TT + 1) * P
                        dve.wait_ge(probs_turned, 8 * p + i + 1)
                        dve.wait_ge(scores_done, 8 * p + i + 1)
                        dve.sem_inc(scores_taken, 1)
                        dve.tensor_tensor_reduce(probs[:, i % 2, :width], bank[2 + i % 2][:, :width],
                                                 mask[:, SEQ - width:], -1.0, -MASKED,
                                                 ALU.add, ALU.min, small[:, 4, i % 2:i % 2 + 1]) \
                            .then_inc(scores_masked, 1)
                    if i:
                        n = i - 1
                        width = (n % TT + 1) * P
                        dve.wait_ge(exp_done, 8 * p + n + 1)
                        dve.reciprocal(small[:, 6, n % 2:n % 2 + 1], small[:, 5, n % 2:n % 2 + 1]) \
                            .then_inc(dve_order, 1)
                        dve.wait_ge(dve_order, 8 * p + order[0] + n + 1)
                        dve.tensor_scalar(probs[:, n % 2, :width], probs[:, n % 2, :width],
                                          small[:, 6, n % 2:n % 2 + 1], None, ALU.mult).then_inc(probs_ready, 1)
                if not last:
                    stage_head(p + 1, 0)
                dve.wait_ge(attn_hi_ready, p + 1)
                dve.tensor_tensor(attn_lo[:, bass.ds(p, 1)].rearrange("p a t -> p (a t)"), bank[6][:],
                                  attn_hi[:, bass.ds(p, 1)].rearrange("p a t -> p (a t)").bitcast(F32),
                                  ALU.subtract).then_inc(attn_ready, 1)
                if not last:
                    stage_head(p + 1, 1)

            with dve.Fori(0, WC - 1) as p:
                attend_pair(p, False)
            attend_pair(WC - 1, True)
            order[0] += 8 * WC

            with dve.Fori(0, KC // SLOTS) as i:
                for s in range(SLOTS):
                    b = 2 - s % 2 * 2
                    dve.wait_ge(tile_done, T_BRANCH + SLOTS * i + s + 1)
                    dve.scalar_tensor_tensor(out=work[:, s % 2],
                                             in0=gates[:, bass.ds(2 * SLOTS * i + 2 * s, 1)].rearrange("p a t -> p (a t)"),
                                             scalar=1.0, in1=bank[b][:], op0=ALU.add, op1=ALU.mult)
                    dve.scalar_tensor_tensor(out=squares[:, s % 2],
                                             in0=gates[:, bass.ds(2 * SLOTS * i + 2 * s + 1, 1)].rearrange("p a t -> p (a t)"),
                                             scalar=1.0, in1=bank[b + 1][:], op0=ALU.add, op1=ALU.mult) \
                        .then_inc(branch_read, 1)
                    dve.wait_ge(branch_read, SLOTS * i + s + 1 + 2)
                    dve.tensor_tensor(work[:, s % 2], work[:, s % 2], squares[:, s % 2], ALU.add).then_inc(merged, 1)
                    dve.wait_ge(merged_hi, SLOTS * i + s + 1)
                    dve.scalar_tensor_tensor(out=h_lo[:, bass.ds(SLOTS * i + s, 1)].rearrange("p a t -> p (a t)"),
                                             in0=work[:, s % 2], scalar=0.5,
                                             in1=h_hi[:, bass.ds(SLOTS * i + s, 1)].rearrange("p a t -> p (a t)").bitcast(F32),
                                             op0=ALU.mult, op1=ALU.subtract).then_inc(merged_ready, 1)
                    dve.wait_ge(merged_ready, SLOTS * i + s + 1)

            with dve.Fori(0, KC // SLOTS) as i:
                for s in range(SLOTS):
                    chunk = x[:, bass.ds(SLOTS * i + s, 1)].rearrange("p a t -> p (a t)")
                    dve.wait_ge(tile_done, T_OUT + SLOTS * i + s + 1)
                    dve.scalar_tensor_tensor(out=chunk, in0=bank[4 + s][:],
                                             scalar=mod[:, bass.ds(SLOTS * i + s + GATE_M, 1)], in1=chunk,
                                             op0=ALU.mult, op1=ALU.add).then_inc(mixed_in, 1)
                    add_square(s % 2, KC + SLOTS * i + s + 1)
                    dve.wait_ge(scaled_hi, KC + SLOTS * i + s + 1)
                    dve.scalar_tensor_tensor(
                        out=g_lo[:, bass.ds(SLOTS * i + s + SCALED, 1)].rearrange("p a t -> p (a t)"),
                        in0=chunk, scalar=gain[:, 1, bass.ds(SLOTS * i + s, 1)],
                        in1=g_hi[:, bass.ds(SLOTS * i + s + SCALED, 1)].rearrange("p a t -> p (a t)").bitcast(F32),
                        op0=ALU.mult, op1=ALU.subtract).then_inc(scaled_ready, 1)
            spread_rstd(1, 6)
            norm_chunks(1, SHIFT_F)
            dve.wait_ge(shift_in_bank, 2)
            dve.tensor_copy(shifted[:, 1, 0:2], bank[2][:, 0:2]).then_inc(shifted_ready, 1)
            for half in range(2):
                first_over_rms(WC + half, bank[UP_BANKS[half]], squares[:, half])
            dve.memset(sum_sq[:], 0.0).then_inc(mod_ready, 1)

            def mlp_pairs(i, first):
                for s in range(2):
                    j = 2 * i + s
                    for half, conv in enumerate((conv_act, conv_lin)):
                        product = squares[:, half] if first and s == 0 else bank[4 + 2 * s + half]
                        dve.wait_ge(conv_begun, 2 * j + half + 1)
                        dve.scalar_tensor_tensor(out=conv[:, s, 1:], in0=product[:, :SEQ - 1],
                                                 scalar=cols[:, bass.ds(j + (half * FC + C_WCONV + 2 * FC), 1)],
                                                 in1=conv[:, s, 1:], op0=ALU.mult, op1=ALU.add).then_inc(dve_order, 1)
                        dve.wait_ge(dve_order, 4 * i + (order[0] + 2 * s + half + 1))
                        dve.scalar_tensor_tensor(out=conv[:, s, 2:], in0=product[:, :SEQ - 2],
                                                 scalar=cols[:, bass.ds(j + (half * FC + C_WCONV), 1)],
                                                 in1=conv[:, s, 2:], op0=ALU.mult, op1=ALU.add).then_inc(conv_done, 1)
                    dve.wait_ge(silu_done, j + 1)
                    dve.wait_ge(conv_done, 2 * j + 2 + 4)
                    dve.tensor_tensor(glu[:, s], conv_act[:, s], conv_lin[:, s], ALU.mult).then_inc(glu_ready, 1)
                    dve.wait_ge(g_hi_ready, j + 1)
                    dve.tensor_tensor(g_lo[:, bass.ds(j, 1)].rearrange("p a t -> p (a t)"), glu[:, s],
                                      g_hi[:, bass.ds(j, 1)].rearrange("p a t -> p (a t)").bitcast(F32),
                                      ALU.subtract).then_inc(g_ready, 1)
                    dve.wait_ge(g_ready, j + 1)

            mlp_pairs(0, True)
            with dve.Fori(1, FC // 2) as i:
                mlp_pairs(i, False)
            order[0] += 2 * FC

            def down_chunk(c, s):
                chunk = x[:, bass.ds(c, 1)].rearrange("p a t -> p (a t)")
                dve.wait_ge(tile_done, T_DOWN + 2 * c + 2)
                dve.scalar_tensor_tensor(out=chunk, in0=bank[s][:], scalar=mod[:, bass.ds(c + GATE_F, 1)], in1=chunk,
                                         op0=ALU.mult, op1=ALU.add).then_inc(down_added, 1)

            with dve.Fori(0, KC // 2 - 1) as i:
                for s in range(2):
                    down_chunk(2 * i + s, s)
                    add_square(s, 2 * KC + 2 * i + s + 1)
            down_chunk(KC - 2, 0)
            add_square(0, 3 * KC - 1)
            down_chunk(KC - 1, 1)
            spread_rstd(2, 2)
            dve.wait_ge(rstd_ready, 3)
            for c in (c for c in range(KC) if c not in POOL_OUT):
                dve.scalar_tensor_tensor(out=x[:, c], in0=x[:, c], scalar=cols[:, C_GFIN + c:C_GFIN + c + 1],
                                         in1=rstd[:], op0=ALU.mult, op1=ALU.mult).then_inc(out_ready, 1)

        @block.tensor
        def _(pe):
            def product(out_ap, left, right, left_cols, right_cols, first, last):
                passes = [(0, 0), (0, 1), (1, 0)]
                for n, (a, b) in enumerate(passes):
                    ins = pe.matmul(out_ap, left[a][left_cols], right[b][right_cols],
                                    start=first and n == 0, stop=last and n == 2)
                return ins

            w, h = (w_hi, w_lo), (h_hi, h_lo)

            def block_cols(slot, k):
                return (slice(None), slice(slot * TILE + k * P, slot * TILE + (k + 1) * P))

            def chunk(k):
                return (slice(None), k)

            def token_stats(n, stat_bank):
                pe.wait_ge(square_added, KC * (n + 1) + 2)
                for t in range(TT):
                    ins = pe.matmul(bank[stat_bank][:, t:t + 1], sum_sq[:, t * P:(t + 1) * P], ones[:, 0:1],
                                    start=True, stop=True)
                ins.then_inc(stats_done, 1)

            def spread(n, spread_bank):
                for t in range(TT):
                    pe.wait_ge(diag_ready, TT * n + t + 1)
                    pe.matmul(bank[spread_bank][:, t * P:(t + 1) * P], ones[:], diag[:, t * P:(t + 1) * P],
                              start=True, stop=True).then_inc(rstd_spread, 1)

            def mod_columns(group):
                if group < SHARED:
                    pe.wait_ge(mod_half_summed, group + 1)
                    pe.wait_ge(mod_row_ready, group + 1)
                else:
                    pe.wait_ge(mod_half_summed, 2 * group + 2 - SHARED)
                for m in range(4):
                    col = bank[7][:, MOD_ORDER[group] * 4 + m:MOD_ORDER[group] * 4 + m + 1]
                    ins = pe.matmul(col, mod_acc[:, group % ACCS, m * P:(m + 1) * P], ones[:, 0:1],
                                    start=True, stop=group >= SHARED)
                    if group < SHARED:
                        ins = pe.matmul(col, mod_row[0:1, m * P:(m + 1) * P], ones[0:1, 0:1], start=False, stop=True)
                ins.then_inc(mod_in_bank, 1)

            pe.sem_inc(probs_turned, 2)
            pe.sem_inc(head_done, 1)
            pe.wait_ge(c_ready, 1)
            wait_mod_landed(pe, 1)
            for r in range(4):
                ins = pe.matmul(bank[6][0:1, :], c_act[:, 4 + r:5 + r], mod_half(1)[:, r], start=r == 0, stop=r == 3)
            ins.then_inc(mod_half_multiplied, 1)
            pe.wait_ge(consts_built, 2)
            for group in range(EARLY // 2):
                mod_columns(group)

            def weights_times_shift(n, slots, in_bank):
                for k in range(KC):
                    for part in range(2):
                        ins = pe.matmul(in_bank[0:2, :slots * P], shift_parts[:, n, k],
                                        w[part][:, :slots * TILE].rearrange("p (s k m) -> p s k m", s=slots, m=P)[:, :, k],
                                        start=k == 0 and part == 0, stop=k == KC - 1 and part == 1)
                return ins

            def turn_shift_row(n, slots, row, in_bank):
                pe.wait_ge(shift_row_ready, n + 1)
                for c in range(slots):
                    ins = pe.matmul(in_bank[:, c:c + 1], row[:, c * P:(c + 1) * P], ones[0:2, 0:1], start=True, stop=True)
                ins.then_inc(shift_in_bank, 1)

            pe.wait_ge(lo_ready, 2)
            for k in range(KC):
                pe.wait_ge(scaled_ready, k + 1)
                for t in range(2):
                    ins = product(bank[Q_BANKS[t]][:], w, h, block_cols(t, k), chunk(k), k == 0, k == KC - 1)
                    if k == KC - 1:
                        ins.then_inc(first_done, 1)
            token_stats(0, 2)
            for t in range(2, 4):
                pe.wait_ge(lo_ready, t + 1)
                for k in range(KC):
                    ins = product(bank[Q_BANKS[t]][:], w, h, block_cols(t, k), chunk(k), k == 0, k == KC - 1)
                    if k == KC - 1:
                        ins.then_inc(first_done if t == 2 else tile_done, 1)
                    elif t == 3:
                        ins.then_inc(scaled_used, 1)
                        if k == 2:
                            for group in range(EARLY // 2, EARLY):
                                mod_columns(group)
                        if k == 3:
                            spread(0, 1)
                            pe.wait_ge(shift_ready, 1)
                            weights_times_shift(0, WC, bank[6]).then_inc(tile_done, 3)

            for t in range(T_VS, T_K):
                pe.wait_ge(lo_ready, t + 1)
                for kk in range(2):
                    k = t % 4 * 2 + kk
                    if t < T_V:
                        pe.wait_ge(h_ready, k + 1)
                    for n in range(TT):
                        if t == T_VS and kk == 0 and n == 1:
                            pe.wait_ge(rstd_ready, 1)
                        if t == T_VS and kk == 0 and n in Q_BANKS:
                            pe.wait_ge(first_scaled, Q_BANKS.index(n) + 1)
                        if t == T_V and kk == 0 and n == 2:
                            pe.wait_ge(shifted_ready, 1)
                        if t == T_V and kk == 0 and n == 3:
                            pe.wait_ge(vs_ready, 1)
                        cols_w = (slice(None), slice(t % SLOTS * TILE + kk * 512, t % SLOTS * TILE + (kk + 1) * 512))
                        ins = product(bank[n if t < T_V else V_BANKS[n]][:], h, w,
                                      (slice(None), k, slice(n * P, (n + 1) * P)), cols_w,
                                      k == 0, k == KC - 1)
                ins.then_inc(tile_done, 1)
                if t == T_VS:
                    turn_shift_row(0, WC, mod_row[0:2, :], bank[6])
                if t in MOD_AFTER:
                    mod_columns(EARLY + MOD_AFTER.index(t))

            for t in range(T_K, T_GATES):
                pe.wait_ge(lo_ready, t + 1)
                if t == T_K:
                    pe.wait_ge(vs_ready, TT)
                elif t == T_U:
                    pe.wait_ge(v_ready, TT)
                elif t % SLOTS >= 2:
                    pe.wait_ge(proj_ready, WC + t - T_K - 1)
                for k in range(KC):
                    ins = product(bank[(1 if t < T_U else 4) + t % 2][:], w, h, block_cols(t % SLOTS, k), chunk(k), k == 0, k == KC - 1)
                ins.then_inc(tile_done, 1)
                if t in MOD_AFTER:
                    mod_columns(EARLY + MOD_AFTER.index(t))
                if t == T_U - 1:
                    pe.wait_ge(spatial_masked, 1)
                    pe.wait_ge(vs_normed, TT)
                    pe.wait_ge(v_ready, TT)
                    for c in range(WC):
                        if c in (1, 2):
                            pe.wait_ge(proj_ready, 2 * WC - 2 + c)
                        for e in range(2):
                            g = 2 * c + e
                            for n in range(TT):
                                ins = pe.matmul(bank[c][64 * e:64 * e + 64, n * P:(n + 1) * P],
                                                vs[:, n, g * 64:(g + 1) * 64], w_spatial[:, g, :],
                                                start=True, stop=True)
                        ins.then_inc(spatial_done, 1)

            pe.wait_ge(mix_ready, WC)
            step_units = [3, 3, 3, 3, 3, 3, 3, 3, 3, 2, 3]
            with pe.Fori(0, WC) as p:
                unit = 0
                for i in range(11):
                    for _ in range(step_units[i]):
                        j, k = unit // UNITS, unit % UNITS
                        if k == 0:
                            pe.wait_ge(lo_ready, T_GATES + 4 * p + j + 1)
                            pe.wait_ge(gate_ready, 4 * p + j + 1)
                        ins = product(bank[j % 2][:], w, h, block_cols(j, k), chunk(k), k == 0, k == KC - 1)
                        if k == KC - 1:
                            ins.then_inc(tile_done, 1)
                        unit += 1
                    if i < 8:
                        e, qb = i // TT, i % TT
                        width = (qb + 1) * P
                        rows = slice(64 * e, 64 * e + 64)
                        if qb == 0:
                            pe.wait_ge(head_staged, 6 * p + 3 * e + 3)
                        pe.wait_ge(scores_masked, 8 * p + i + 1)
                        queries = slice(qb * P, width)
                        pe.matmul(bank[2 + i % 2][:, :width], q_parts[:, e, queries], k_twice[:, e, :width],
                                  start=True, stop=False)
                        pe.matmul(bank[2 + i % 2][:, :width], q_parts[rows, e, queries], k_lo[rows, :width],
                                  start=False, stop=True).then_inc(scores_done, 1)
                    if i in (6, 10):
                        e = (i - 6) // 4
                        pe.wait_ge(probsT_ready, 8 * p + 4 * e + 4 + 2)
                        if e == 0:
                            pe.wait_ge(v_staged, p + 1)
                            pe.wait_ge(attn_ready, p + 1)
                        for kb in range(TT):
                            ins = pe.matmul(bank[6][64 * e:64 * e + 64, kb * P:], v_pair[:, kb, 64 * e:64 * e + 64],
                                            probsT[:, kb, kb * P:], start=kb == 0, stop=kb == TT - 1)
                        ins.then_inc(head_done, 1)
                    if 2 <= i < 10:
                        n, qb = i - 2, (i - 2) % TT
                        if n == 0:
                            pe.wait_ge(proj_ready, 3 * WC)
                        pe.wait_ge(probs_ready, 8 * p + n + 1)
                        pe.wait_ge(probsT_ready, 8 * p + n + 1)
                        for kb in range(qb + 1):
                            ins = pe.transpose(bank[4 + n % 2][:, kb * P:(kb + 1) * P],
                                               probs[:, n % 2, kb * P:(kb + 1) * P], ident[:])
                        ins.then_inc(probs_turned, 1)

            pe.wait_ge(scores_masked, 8 * WC + 2)
            pe.wait_ge(sgu_ready, WC)
            with pe.Fori(0, KC // SLOTS) as i:
                for s in range(SLOTS):
                    pe.wait_ge(lo_ready, T_BRANCH + SLOTS * i + s + 1)
                    pe.wait_ge(branch_read, SLOTS * i + s + 1)
                    if s == 1:
                        pe.wait_ge(gate_ready, 2 * KC + 2)
                    for k in [*range(WC, 2 * WC), *range(WC)]:
                        if s == 0 and k == 0:
                            pe.wait_ge(attn_ready, WC + 1)
                        branch = (attn_hi, attn_lo) if k < WC else (sgu_hi, sgu_lo)
                        ins = product(bank[2 - s % 2 * 2 + k // WC][:], w, branch, block_cols(s, k), chunk(k % WC),
                                      k % WC == 0, k % WC == WC - 1)
                    ins.then_inc(tile_done, 1)

            pe.wait_ge(probsT_ready, 8 * WC + 2)
            pe.wait_ge(mod_ready, 3)
            with pe.Fori(0, KC // SLOTS) as i:
                for s in range(SLOTS):
                    pe.wait_ge(lo_ready, T_OUT + SLOTS * i + s + 1)
                    pe.wait_ge(mixed_in, SLOTS * i + s + 1)
                    for k in range(KC):
                        if s == 0:
                            pe.wait_ge(merged_ready, k + 1)
                        ins = product(bank[4 + s][:], w, h, block_cols(s, k), chunk(k), k == 0, k == KC - 1)
                    ins.then_inc(tile_done, 1)
            pe.wait_ge(branch_read, KC + 2)
            pe.wait_ge(lo_ready, T_UP + 2)
            for k in range(KC):
                pe.wait_ge(scaled_ready, KC + k + 1)
                for s in range(2):
                    ins = product(bank[UP_BANKS[s]][:], w, (g_hi, g_lo), block_cols(s, k), chunk(SCALED + k),
                                  k == 0, k == KC - 1)
                    if k == KC - 1:
                        ins.then_inc(first_done, 1)
                if k == 2:
                    token_stats(1, 6)
                if k == 4:
                    spread(1, 1)
            pe.wait_ge(shift_ready, 2)
            weights_times_shift(1, 2, bank[2]).then_inc(tile_done, 2)
            pe.wait_ge(mixed_in, KC + 4)
            pe.wait_ge(lo_ready, T_UP + 4)
            for k in range(KC):
                pe.wait_ge(h_ready, KC + k + 1)
                for s in range(2, SLOTS):
                    ins = product(bank[4 + s][:], w, h, block_cols(s, k), chunk(k), k == 0, k == KC - 1)
                    if k == KC - 1:
                        ins.then_inc(tile_done, 1)
                if k == 4:
                    turn_shift_row(1, 2, glu[0:2, 0], bank[2])

            def up_tiles(i):
                for s in range(SLOTS):
                    pe.wait_ge(lo_ready, T_UP + SLOTS * i + s + 1)
                    if not (isinstance(i, int) and s < 2):
                        pe.wait_ge(conv_done, SLOTS * i + s + 1)
                    for k in range(KC):
                        ins = product(bank[4 + s][:], w, h, block_cols(s, k), chunk(k), k == 0, k == KC - 1)
                    ins.then_inc(tile_done, 1)

            up_tiles(1)
            with pe.Fori(2, FC // 2) as i:
                up_tiles(i)

            pe.wait_ge(g_ready, FC - 1)
            with pe.Fori(0, KC // 2) as i:
                for s in range(2):
                    pe.wait_ge(down_added, 2 * i + s + 1)
                    for half in range(2):
                        pe.wait_ge(lo_ready, T_DOWN + 4 * i + 2 * s + half + 1)
                        for r in range(DOWN_UNITS):
                            k = half * DOWN_UNITS + r
                            if k == FC - 1 and s == 0:
                                pe.wait_ge(g_ready, FC)
                            ins = product(bank[s][:], w, (g_hi, g_lo), block_cols(2 * half, r), chunk(k),
                                          k == 0, k == FC - 1)
                        ins.then_inc(tile_done, 1)
            for last, source in enumerate((sum_sq, squares[:, 1])):
                if last:
                    pe.wait_ge(squared, 3 * KC)
                else:
                    pe.wait_ge(square_added, 3 * KC - 1 + 2)
                for t in range(TT):
                    ins = pe.matmul(bank[2][:, 2 * t + last:2 * t + last + 1], source[:, t * P:(t + 1) * P],
                                    ones[:, 0:1], start=True, stop=True)
            ins.then_inc(stats_done, 1)
            spread(2, 3)


def kernel(**inputs):
    import numpy as np
    import concourse.bacc as bacc
    from concourse.bass_utils import run_bass_kernel_spmd

    def a(name):
        return np.asarray(inputs[name])

    def columns(v):
        return v.reshape(-1, P).T

    def by_columns(w):
        k, n = w.shape
        return w.reshape(k // P, P, n // P, P).transpose(2, 1, 0, 3).reshape(n // P, P, k)

    def by_rows(w):
        k, n = w.shape
        return w.reshape(k // (2 * P), 2, P, n).transpose(0, 2, 1, 3).reshape(k // (2 * P), P, 2 * n)

    def alternate(one, other):
        return np.stack([one, other], axis=1).reshape(-1, *one.shape[1:])

    w_in = a("w_in")[0]
    q, k, v, u, vs = (w_in[:, n * WIDTH:(n + 1) * WIDTH] for n in range(5))
    gate_a, gate_s = (w_in[:, 5 * WIDTH + n * D_MODEL:5 * WIDTH + (n + 1) * D_MODEL] for n in range(2))
    branches = np.concatenate([by_columns(a("w_attn_br")[0]), by_columns(a("w_sgu_br")[0])], axis=2)
    w_up = a("w_up")[0]
    tiles = np.concatenate([
        by_columns(q), by_rows(vs), by_rows(v), by_columns(k), by_columns(u),
        alternate(by_columns(gate_a), by_columns(gate_s)), branches, by_columns(a("w_out")[0]),
        alternate(by_columns(w_up[:, :D_FF]), by_columns(w_up[:, D_FF:]))])
    down = by_columns(a("w_down")[0]).reshape(KC, P, 2, DOWN_TILE).transpose(0, 2, 1, 3).reshape(N_DOWN, P, DOWN_TILE)
    arrays = {
        "xT": a("x")[0].T,
        "columns": np.concatenate([columns(a(n).reshape(-1)) for n in
                                   ("c", "b_mod", "g_mix", "g_ffn", "g_final", "w_conv", "b_conv")], axis=1),
        "w_mod": a("w_mod")[0],
        "tiles": tiles,
        "down_tiles": down,
        "w_sgu": a("w_sgu_s")[0].transpose(2, 0, 1),
        "g_sgu": a("g_sgu"),
        "b_sgu": a("b_sgu_s")[0],
    }
    arrays = {name: np.ascontiguousarray(v) for name, v in arrays.items()}
    nc = bacc.Bacc("TRN2", target_bir_lowering=False, num_devices=1, dynamic_dma_scratch_size=1024)
    aps = [nc.dram_tensor(name, v.shape, mybir.dt.from_np(v.dtype), kind="ExternalInput").ap()
           for name, v in arrays.items()]
    out = nc.dram_tensor("outT", (D_MODEL, SEQ), F32, kind="ExternalOutput").ap()
    decoder_layer(nc, *aps, out)
    r = run_bass_kernel_spmd(nc, [arrays], core_ids=[0])
    return np.ascontiguousarray(r.results[0]["outT"].T)[None]
```

```python
from contextlib import ExitStack

import concourse.bass as bass
from concourse import mybir

P = 128
D_MODEL, SEQ, HEADS, HEAD_DIM = 1024, 512, 8, 64
WIDTH = HEADS * HEAD_DIM
GROUPS = 8
D_FF = 2816
EPS = 1e-6
KC = D_MODEL // P
WC = WIDTH // P
FC = D_FF // P
TT = SEQ // P

T_Q, T_VS, T_V, T_K, T_U = 0, 4, 8, 12, 16
T_GATES = 20
T_BRANCH = T_GATES + 2 * KC
T_OUT = T_BRANCH + KC
T_UP = T_OUT + KC
T_DOWN = T_UP + 2 * FC
UNITS, DOWN_UNITS = 8, FC // 2
TILE, DOWN_TILE = UNITS * P, DOWN_UNITS * P
SLOTS = 4
N_DOWN = 2 * KC
POOL_BLOCKS = 5
STATS_AT, SPREAD_AT = 4, 11
HALF = SEQ // 2
POOL_OUT = (1, 3, 5)

C_C = 0
C_BMOD = C_C + KC
C_GMIX = C_BMOD + 6 * KC
C_GFFN = C_GMIX + KC
C_GFIN = C_GFFN + KC
C_WCONV = C_GFIN + KC
C_BCONV = C_WCONV + 3 * 2 * FC
N_COLS = C_BCONV + 2 * FC
SCALED = KC
SHIFT_M, SCALE_M, GATE_M, SHIFT_F, SCALE_F, GATE_F = (KC * n for n in range(6))
MOD_ORDER = [2, 3, 0, 1, 4, 5, 6, 7, 8, 9, 10, 11]
ROW_HALF = 1
EARLY = 4
MOD_BUFS = 4
ACCS = EARLY
LATE = len(MOD_ORDER) - EARLY
LATE_AFTER = T_GATES - 2
LATE_HALVES_BEHIND = {11: 2, 12: 1, 13: 1, 15: 2, 16: 2, 18: 2, 19: 2}
BLOCK = 32
Q_BANKS = [4, 5, 0, 3]
V_BANKS = [4, 5, 6, 0]
DOWN_BANKS = [1, 4]
SPREAD_BANKS = [3, 5]
UP_BANKS = [0, 3]

MASKED = -3.0e38
F32 = mybir.dt.float32
F32R = mybir.dt.float32r
BF16 = mybir.dt.bfloat16
ALU = mybir.AluOpType
ACT = mybir.ActivationFunctionType


def decoder_layer(nc, xT, cols_in, w_mod, tiles, down_tiles, w_sgu, g_sgu, b_sgu, out):
    with ExitStack() as ctx:
        def sem(name):
            return ctx.enter_context(nc.semaphore(name))

        def held(scope):
            return lambda name, shape, dt=F32: scope.enter_context(nc.sbuf_tensor(name, shape, dt))

        sb = held(ctx)
        x = sb("x", [P, KC, SEQ])
        h_hi = sb("h_hi", [P, KC, SEQ], F32R)
        h_lo = sb("h_lo", [P, KC, SEQ], F32R)
        raw = sb("raw", [P, SLOTS * TILE])
        w_hi = sb("w_hi", [P, SLOTS * TILE], F32R)
        w_lo = sb("w_lo", [P, SLOTS * TILE], F32R)
        cols = sb("cols", [P, N_COLS])
        c_act = sb("c_act", [P, KC])
        mod = sb("mod", [P, 6 * KC])
        gain = sb("gain", [P, 2, KC])
        shift_parts = sb("shift_parts", [P, 2, KC, 2], F32R)
        shifted = sb("shifted", [P, 2, WC])
        rstd = sb("rstd", [P, SEQ])
        small = sb("small", [P, 8, TT])
        ident = sb("ident", [P, P])
        ones = sb("ones", [P, P])
        mask = sb("mask", [P, SEQ], BF16)
        work = sb("work", [P, 2, SEQ])
        squares = sb("squares", [P, 2, SEQ])
        sum_sq = sb("sum_sq", [P, SEQ])
        diag = sum_sq
        probs = squares
        bank = [ctx.enter_context(nc.psum_tensor(f"bank{n}", [P, 512], F32)) for n in range(8)]

        with ExitStack() as mixing:
            sb = held(mixing)
            v = sb("v", [P, TT, WIDTH])
            qT = sb("qT", [P, WC, SEQ])
            kT = sb("kT", [P, WC, SEQ])
            with ExitStack() as early:
                sb = held(early)
                vs = sb("vs", [P, TT, WIDTH])
                mix = sb("mix", [P, WC, SEQ])
                u = sb("u", [P, 2, SEQ])
                w_spatial = sb("w_spatial", [P, GROUPS, P])
                g_row = sb("g_row", [P, WIDTH])
                b_row = sb("b_row", [P, WC, P])
                select = sb("select", [P, 7 * BLOCK])
                partial = sb("partial", [P, LATE, 512 // BLOCK])
                mod_w = sb("mod_w", [P, MOD_BUFS, 4, 512])
                mod_acc = sb("mod_acc", [P, ACCS, 512])
                mod_row = sb("mod_row", [P, 512])
            with ExitStack() as late:
                sb = held(late)
                gates = sb("gates", [P, 2 * KC, SEQ])
                attn_hi = sb("attn_hi", [P, WC, SEQ], F32R)
                attn_lo = sb("attn_lo", [P, WC, SEQ], F32R)
                sgu_hi = sb("sgu_hi", [P, WC, SEQ], F32R)
                sgu_lo = sb("sgu_lo", [P, WC, SEQ], F32R)
                q_parts = sb("q_parts", [P, 2, SEQ], F32R)
                k_lo = sb("k_lo", [P, SEQ], F32R)
                k_twice = sb("k_twice", [P, 2, SEQ], F32R)
                v_pair = sb("v_pair", [P, TT, P])
                probsT = sb("probsT", [P, TT, SEQ])
        with ExitStack() as mlp:
            sb = held(mlp)
            g_hi = sb("g_hi", [P, FC, SEQ], F32R)
            g_lo = sb("g_lo", [P, FC, SEQ], F32R)
            conv_act = sb("conv_act", [P, 2, SEQ])
            conv_lin = sb("conv_lin", [P, 2, SEQ])
            glu = sb("glu", [P, 2, SEQ])

        x_landed = [sem(f"x_landed{n}") for n in range(4)]
        cols_landed = sem("cols_landed")
        sgu_landed = sem("sgu_landed")
        mod_landed = [sem(f"mod_landed{n}") for n in range(2 * EARLY)]
        raw_landed = [sem(f"raw_landed{n}") for n in range(SLOTS)]
        out_landed = sem("out_landed")
        consts_built = sem("consts_built")
        pool_order = sem("pool_order")
        spatial_masked = sem("spatial_masked")
        hi_ready = sem("hi_ready")
        lo_ready = sem("lo_ready")
        tile_done = sem("tile_done")
        c_ready = sem("c_ready")
        mod_half_summed = sem("mod_half_summed")
        mod_half_multiplied = sem("mod_half_multiplied")
        mod_row_ready = sem("mod_row_ready")
        late_summed = sem("late_summed")
        mod_in_bank = sem("mod_in_bank")
        mod_ready = sem("mod_ready")
        squared = sem("squared")
        square_added = sem("square_added")
        stats_done = sem("stats_done")
        mean_ready = sem("mean_ready")
        root_ready = sem("root_ready")
        diag_ready = sem("diag_ready")
        rstd_spread = sem("rstd_spread")
        rstd_ready = sem("rstd_ready")
        scaled_hi = sem("scaled_hi")
        scaled_ready = sem("scaled_ready")
        scaled_used = sem("scaled_used")
        shift_ready = sem("shift_ready")
        first_done = sem("first_done")
        first_scaled = sem("first_scaled")
        shift_row_ready = sem("shift_row_ready")
        shift_in_bank = sem("shift_in_bank")
        shifted_ready = sem("shifted_ready")
        normed = sem("normed")
        h_hi_ready = sem("h_hi_ready")
        h_ready = sem("h_ready")
        vs_ready = sem("vs_ready")
        v_ready = sem("v_ready")
        proj_ready = sem("proj_ready")
        vs_mean_ready = sem("vs_mean_ready")
        vs_root_ready = sem("vs_root_ready")
        vs_normed = sem("vs_normed")
        spatial_done = sem("spatial_done")
        mix_ready = sem("mix_ready")
        gated = sem("gated")
        sgu_hi_ready = sem("sgu_hi_ready")
        sgu_ready = sem("sgu_ready")
        head_hi = sem("head_hi")
        head_staged = sem("head_staged")
        v_staged = sem("v_staged")
        scores_done = sem("scores_done")
        scores_masked = sem("scores_masked")
        scores_taken = sem("scores_taken")
        exp_done = sem("exp_done")
        probs_ready = sem("probs_ready")
        probs_turned = sem("probs_turned")
        probsT_ready = sem("probsT_ready")
        head_done = sem("head_done")
        attn_hi_ready = sem("attn_hi_ready")
        attn_ready = sem("attn_ready")
        gate_ready = sem("gate_ready")
        branch_read = sem("branch_read")
        merged = sem("merged")
        merged_hi = sem("merged_hi")
        merged_ready = sem("merged_ready")
        mixed_in = sem("mixed_in")
        pair_shifted = sem("pair_shifted")
        conv_begun = sem("conv_begun")
        conv_done = sem("conv_done")
        silu_done = sem("silu_done")
        glu_ready = sem("glu_ready")
        g_hi_ready = sem("g_hi_ready")
        g_ready = sem("g_ready")
        down_added = sem("down_added")
        last_lo_ready = sem("last_lo_ready")
        half_done = sem("half_done")
        half_added = sem("half_added")
        half_squared = sem("half_squared")
        dve_order = sem("dve_order")
        out_ready = sem("out_ready")
        pool_out_ready = sem("pool_out_ready")

        mod_view = w_mod.rearrange("(k p) n -> p k n", p=P)
        out_view = out.rearrange("(c p) t -> p c t", p=P)

        early_bufs = [mod_w[:, n] for n in range(MOD_BUFS)] + [v, qT, kT, mix]

        def mod_half(n):
            return early_bufs[n] if n < 2 * EARLY else mod_w[:, n % MOD_BUFS]

        def wait_mod_landed(engine, n):
            if n < 2 * EARLY:
                engine.wait_ge(mod_landed[n], 16)
            else:
                engine.wait_ge(mod_landed[n % MOD_BUFS], 16 * (n // MOD_BUFS))

        def summed(n):
            return n + 1 if n < ROW_HALF else n

        def raw_slot(tile):
            return raw[:, tile % SLOTS * TILE:(tile % SLOTS + 1) * TILE]

        def part_slot(part, slot):
            return part[:, slot * TILE:(slot + 1) * TILE]

        def down_slot(part, n):
            return part[:, n % 2 * 2 * TILE:n % 2 * 2 * TILE + DOWN_TILE]

        block = ctx.enter_context(nc.Block())

        @block.sync
        def _(sp):
            def load_mod_half(n):
                last = n - MOD_BUFS if n >= 2 * EARLY + MOD_BUFS else n - 2 * EARLY
                if last == ROW_HALF:
                    sp.wait_ge(mod_half_multiplied, 1)
                elif last >= 0:
                    sp.wait_ge(mod_half_summed, summed(last))
                early = n < 2 * EARLY
                g = MOD_ORDER[n // 2 if early else EARLY + (n - 2 * EARLY) // 4 * 2 + n % 2]
                rows = (n % 2 if early else n // 2 % 2) * 4
                sp.dma_start(mod_half(n)[:], mod_view[:, rows:rows + 4, g * 512:(g + 1) * 512]) \
                    .then_inc(mod_landed[n if n < 2 * EARLY else n % MOD_BUFS], 16)

            def load_tile(t):
                if t >= SLOTS:
                    sp.wait_ge(lo_ready, t - SLOTS + 1)
                sp.dma_start(raw_slot(t), tiles[t]).then_inc(raw_landed[t % SLOTS], 16)

            sp.dma_start(cols[:], cols_in).then_inc(cols_landed, 16)
            for n in range(EARLY):
                load_mod_half(n)
            load_tile(0)
            load_tile(1)
            for n in range(4):
                chunks = slice(n * KC // 4, (n + 1) * KC // 4)
                sp.dma_start(x[:, chunks], xT.rearrange("(c p) t -> p c t", p=P)[:, chunks]).then_inc(x_landed[n], 16)
            for n in range(EARLY, 2 * EARLY):
                load_mod_half(n)
                if n in (2 * EARLY - 3, 2 * EARLY - 2):
                    load_tile(n - 3)
            for t in range(SLOTS, 2 * SLOTS):
                load_mod_half(t + SLOTS)
                load_tile(t)
            sp.dma_start(w_spatial[:], w_sgu).then_inc(sgu_landed, 16)
            sp.dma_start(g_row[:], bass.AP(tensor=g_sgu.tensor, offset=0, ap=[[0, P], [1, WIDTH]])) \
                .then_inc(sgu_landed, 16)
            for half in range(2):
                sp.dma_start(b_row[64 * half:64 * half + 64],
                             bass.AP(tensor=b_sgu.tensor, offset=half * P, ap=[[0, 64], [2 * P, WC], [1, P]])) \
                    .then_inc(sgu_landed, 16)
            n = 2 * EARLY + MOD_BUFS
            for t in range(2 * SLOTS, 5 * SLOTS):
                load_tile(t)
                for _ in range(LATE_HALVES_BEHIND.get(t, 0)):
                    load_mod_half(n)
                    n += 1
            with sp.Fori(5, T_DOWN // SLOTS) as i:
                for s in range(SLOTS):
                    sp.wait_ge(lo_ready, SLOTS * i + s - SLOTS + 1)
                    sp.dma_start(raw_slot(s), tiles[bass.ds(SLOTS * i + s, 1)].rearrange("a p n -> p (a n)")) \
                        .then_inc(raw_landed[s], 16)
            for n in range(2):
                sp.wait_ge(lo_ready, T_DOWN - 2 + 2 * n)
                sp.dma_start(down_slot(raw, n), down_tiles[n]).then_inc(raw_landed[2 * n], 16)
            with sp.Fori(1, N_DOWN // 2) as i:
                for n in range(2):
                    sp.wait_ge(lo_ready, T_DOWN + 2 * i + n - 1)
                    sp.dma_start(down_slot(raw, n), down_tiles[bass.ds(2 * i + n, 1)].rearrange("a p n -> p (a n)")) \
                        .then_inc(raw_landed[2 * n], 16)
            for half in range(2):
                tokens = slice(half * HALF, (half + 1) * HALF)
                for c in range(0, KC, 2):
                    pools = sum(n < c + 2 for n in POOL_OUT)
                    sp.wait_ge(out_ready, half * (KC - len(POOL_OUT)) + c + 2 - pools)
                    if pools:
                        sp.wait_ge(pool_out_ready, half * len(POOL_OUT) + pools)
                    sp.dma_start(out_view[:, c:c + 2, tokens], x[:, c:c + 2, tokens]).then_inc(out_landed, 16)
            sp.wait_ge(out_landed, 16 * KC)

        @block.gpsimd
        def _(pool):
            pool.memset(ones[:], 1.0).then_inc(pool_order, 1)
            pool.memset(mask[:], 0.0).then_inc(pool_order, 1)
            pool.memset(sum_sq[:], 0.0).then_inc(pool_order, 1)
            pool.wait_ge(pool_order, 3)
            pool.affine_select(out=ident[:], in_=ones[:], compare_op=ALU.is_equal, fill=0.0, base=0,
                               pattern=[[-1, P]], channel_multiplier=1).then_inc(consts_built, 1)
            pool.affine_select(out=mask[:], in_=mask[:], compare_op=ALU.is_ge, fill=MASKED, base=3 * P,
                               pattern=[[-1, SEQ]], channel_multiplier=1).then_inc(consts_built, 1)
            pool.memset(select[:], 0.0).then_inc(pool_order, 1)
            pool.wait_ge(pool_order, 4)
            for n in range(P // BLOCK):
                pool.affine_select(out=select[:, 3 * BLOCK:4 * BLOCK], in_=select[:, 3 * BLOCK:4 * BLOCK],
                                   compare_op=ALU.not_equal, fill=1.0, base=-n * BLOCK, pattern=[[-1, BLOCK]],
                                   channel_multiplier=1).then_inc(consts_built, 1)
                pool.wait_ge(consts_built, 3 + n)
            def split_tiles(i, slots=range(SLOTS)):
                for s in slots:
                    pool.wait_ge(hi_ready, SLOTS * i + s + 1)
                    pool.tensor_tensor(part_slot(w_lo, s), raw_slot(s), part_slot(w_hi, s).bitcast(F32),
                                       ALU.subtract).then_inc(lo_ready, 1)

            split_tiles(0, (0, 1))
            pool.wait_ge(pool_order, 3)
            for c in range(KC):
                pool.wait_ge(squared, c + 1)
                pool.tensor_tensor(sum_sq[:], sum_sq[:], squares[:, c % 2], ALU.add).then_inc(square_added, 1)
                pool.wait_ge(square_added, c + 1 + 2)
            split_tiles(0, (2, 3))
            split_tiles(1)
            pool.wait_ge(sgu_landed, 64)
            pool.affine_select(out=w_spatial[:], in_=w_spatial[:], compare_op=ALU.is_ge, fill=0.0, base=0,
                               pattern=[[0, GROUPS], [1, P]], channel_multiplier=-1).then_inc(spatial_masked, 1)
            with pool.Fori(2, T_DOWN // SLOTS) as i:
                split_tiles(i)
            def split_down(i, n, blocks=DOWN_UNITS):
                pool.wait_ge(hi_ready, T_DOWN + 2 * i + n + 1)
                pool.tensor_tensor(down_slot(w_lo, n)[:, :blocks * P], down_slot(raw, n)[:, :blocks * P],
                                   down_slot(w_hi, n)[:, :blocks * P].bitcast(F32), ALU.subtract).then_inc(lo_ready, 1)

            with pool.Fori(0, N_DOWN // 2 - 1) as i:
                for n in range(2):
                    split_down(i, n)
            split_down(N_DOWN // 2 - 1, 0)
            split_down(N_DOWN // 2 - 1, 1, POOL_BLOCKS)
            pool.wait_ge(scaled_hi, 2 * KC + len(POOL_OUT))
            for half in range(2):
                tokens = slice(half * HALF, (half + 1) * HALF)
                pool.wait_ge(rstd_ready, 3 + half)
                for c in POOL_OUT:
                    pool.tensor_tensor(x[:, c, tokens], x[:, c, tokens], rstd[:, tokens], ALU.mult) \
                        .then_inc(pool_out_ready, 1)

        @block.scalar
        def _(act):
            def round_tile(t):
                s = t % SLOTS
                act.wait_ge(raw_landed[s], 16 * (t // SLOTS + 1))
                act.copy(part_slot(w_hi, s), raw_slot(s)).then_inc(hi_ready, 1)

            act.sem_inc(probsT_ready, 2)
            act.sem_inc(gate_ready, 2)
            act.wait_ge(cols_landed, 16)
            act.activation(c_act[:], cols[:, C_C:C_C + KC], ACT.Silu).then_inc(c_ready, 1)
            act.wait_ge(mod_half_multiplied, 1)
            act.copy(mod_row[0:1, :], bank[6][0:1, :]).then_inc(mod_row_ready, 1)
            round_tile(0)
            round_tile(1)
            act.wait_ge(mod_ready, 1)
            for c in range(KC):
                act.wait_ge(x_landed[c // (KC // 4)], 16)
                act.activation(h_hi[:, c], x[:, c], ACT.Copy, scale=gain[:, 0, c:c + 1]).then_inc(scaled_hi, 1)
                act.wait_ge(square_added, c + 1)
                act.activation(squares[:, c % 2], x[:, c], ACT.Square).then_inc(squared, 1)
            round_tile(2)
            round_tile(3)
            act.wait_ge(mean_ready, 1)
            act.activation(small[:, 1], small[:, 0], ACT.Sqrt).then_inc(root_ready, 1)
            act.wait_ge(rstd_spread, TT)
            act.copy(rstd[:], bank[1][:]).then_inc(rstd_ready, 1)

            def norm_hi(n, shift, between):
                for c in range(KC):
                    between(c)
                    act.wait_ge(normed, n * KC + c + 1)
                    if n == 0 and c < KC - 1:
                        act.wait_ge(scaled_used, c + 1)
                    elif n == 0:
                        act.wait_ge(tile_done, T_VS)
                    act.activation(h_hi[:, c], work[:, c % 2], ACT.Identity,
                                   bias=mod[:, shift + c:shift + c + 1]).then_inc(h_hi_ready, 1)

            def round_next_of_q(c):
                if c % 2 == 0:
                    act.wait_ge(tile_done, T_Q + c // 2 + 1)
                    round_tile(T_Q + c // 2 + SLOTS)
                if c == 3:
                    act.copy(mod_row[0:2, :], bank[6][0:2, :]).then_inc(shift_row_ready, 1)

            norm_hi(0, SHIFT_M, round_next_of_q)
            act.wait_ge(shifted_ready, 1)
            for c in range(WC):
                act.activation(qT[:, c], qT[:, c], ACT.Identity, scale=HEAD_DIM ** -0.5,
                               bias=shifted[:, 0, c:c + 1]).then_inc(proj_ready, 1)
            for t in range(T_VS, T_V):
                act.wait_ge(tile_done, t + 1)
                if t == T_V - 1:
                    for n in range(TT):
                        act.activation(vs[:, n], bank[n][:], ACT.Gelu_apprx_tanh).then_inc(vs_ready, 1)
                round_tile(t + SLOTS)
            for t in range(T_V, T_K):
                act.wait_ge(tile_done, t + 1)
                round_tile(t + SLOTS)
                if t == T_V + 1:
                    act.wait_ge(vs_mean_ready, 1)
                    act.activation(small[:, 3], small[:, 2], ACT.Sqrt).then_inc(vs_root_ready, 1)
            for n in range(TT):
                act.copy(v[:, n], bank[V_BANKS[n]][:]).then_inc(v_ready, 1)
            for t in range(T_K, T_U):
                act.wait_ge(tile_done, t + 1)
                act.copy(kT[:, t - T_K], bank[1 + t % 2][:]).then_inc(proj_ready, 1)
                round_tile(t + SLOTS)
            def stage_head(p, e):
                own = slice(64 * e, 64 * e + 64)
                act.copy(q_parts[own, e], qT[own, bass.ds(p, 1)].rearrange("p a t -> p (a t)")).then_inc(head_hi, 1)
                act.copy(k_twice[own, e], kT[own, bass.ds(p, 1)].rearrange("p a t -> p (a t)")).then_inc(head_hi, 1)

            for t in range(T_U, T_GATES):
                c = t - T_U
                if t == T_GATES - 1:
                    act.wait_ge(late_summed, LATE)
                    for e in range(2):
                        stage_head(0, e)
                act.wait_ge(tile_done, t + 1)
                if c >= 2:
                    act.wait_ge(gated, c - 1)
                act.activation(u[:, c % 2], bank[4 + t % 2][:], ACT.Gelu_apprx_tanh).then_inc(proj_ready, 1)
                round_tile(t + SLOTS)
                act.wait_ge(gated, c + 1)
                act.copy(sgu_hi[:, c], mix[:, c]).then_inc(sgu_hi_ready, 1)
            act.wait_ge(sgu_ready, WC)

            def attend_pair(p, last):
                act.wait_ge(head_done, 2 * p + 1)
                act.copy(v_pair[:], v[:, :, bass.ds(p * P, P)]).then_inc(v_staged, 1)
                for i in range(11):
                    if i < 8:
                        act.wait_ge(scores_masked, 8 * p + i + 1 + 2)
                        width = (i % TT + 1) * P
                        act.activation(probs[:, i % 2, :width], probs[:, i % 2, :width], ACT.Exp, scale=-1.0,
                                       bias=small[:, 4, i % 2:i % 2 + 1],
                                       accum_out=small[:, 5, i % 2:i % 2 + 1]).then_inc(exp_done, 1)
                    if 2 <= i < 10:
                        n, qb = i - 2, (i - 2) % TT
                        act.wait_ge(probs_turned, 8 * p + n + 1 + 2)
                        if qb == 0:
                            act.wait_ge(head_done, 2 * p + n // TT + 1)
                        act.copy(probsT[:, :qb + 1, qb * P:(qb + 1) * P],
                                 bank[4 + n % 2][:, :(qb + 1) * P].rearrange("p (k q) -> p k q", q=P)) \
                            .then_inc(probsT_ready, 1)
                    if i == 8 and not last:
                        act.wait_ge(scores_done, 8 * p + 8)
                        stage_head(p + 1, 0)
                    if i in (2, 4, 7, 10):
                        j = (2, 4, 7, 10).index(i)
                        act.wait_ge(tile_done, T_GATES + 4 * p + j + 1)
                        act.activation(gates[:, bass.ds(4 * p + j, 1)].rearrange("p a t -> p (a t)"),
                                       bank[j % 2][:], ACT.Tanh, scale=0.5).then_inc(gate_ready, 1)
                        if j == 3:
                            act.wait_ge(head_done, 2 * p + 2 + 1)
                            act.copy(attn_hi[:, bass.ds(p, 1)].rearrange("p a t -> p (a t)"), bank[6][:]) \
                                .then_inc(attn_hi_ready, 1)
                        act.wait_ge(raw_landed[j], 16 * (p + T_GATES // SLOTS + 2))
                        act.copy(part_slot(w_hi, j), raw_slot(j)).then_inc(hi_ready, 1)
                if not last:
                    stage_head(p + 1, 1)

            with act.Fori(0, WC - 1) as p:
                attend_pair(p, False)
            attend_pair(WC - 1, True)

            with act.Fori(0, KC // SLOTS) as i:
                for s in range(SLOTS):
                    act.wait_ge(tile_done, T_BRANCH + SLOTS * i + s + 1)
                    act.wait_ge(raw_landed[s], 16 * (i + T_BRANCH // SLOTS + 2))
                    act.copy(part_slot(w_hi, s), raw_slot(s)).then_inc(hi_ready, 1)
                    act.wait_ge(merged, SLOTS * i + s + 1)
                    act.activation(h_hi[:, bass.ds(SLOTS * i + s, 1)].rearrange("p a t -> p (a t)"),
                                   work[:, s % 2], ACT.Copy, scale=0.5).then_inc(merged_hi, 1)
            act.wait_ge(mod_ready, 3)
            with act.Fori(0, KC // SLOTS) as i:
                for s in range(SLOTS):
                    act.wait_ge(tile_done, T_OUT + SLOTS * i + s + 1)
                    act.wait_ge(raw_landed[s], 16 * (i + T_OUT // SLOTS + 2))
                    act.copy(part_slot(w_hi, s), raw_slot(s)).then_inc(hi_ready, 1)
                    act.wait_ge(mixed_in, SLOTS * i + s + 1 + 4)
                    act.wait_ge(square_added, KC + SLOTS * i + s + 1)
                    act.activation(squares[:, s % 2], x[:, bass.ds(SLOTS * i + s, 1)].rearrange("p a t -> p (a t)"),
                                   ACT.Square).then_inc(squared, 1)
                    act.activation(g_hi[:, bass.ds(SLOTS * i + s + SCALED, 1)].rearrange("p a t -> p (a t)"),
                                   x[:, bass.ds(SLOTS * i + s, 1)].rearrange("p a t -> p (a t)"), ACT.Copy,
                                   scale=gain[:, 1, bass.ds(SLOTS * i + s, 1)]).then_inc(scaled_hi, 1)
            act.wait_ge(mean_ready, 2)
            act.activation(small[:, 1], small[:, 0], ACT.Sqrt).then_inc(root_ready, 1)
            act.wait_ge(rstd_spread, 2 * TT)
            act.copy(rstd[:], bank[1][:]).then_inc(rstd_ready, 1)

            def round_next_of_up(c):
                if c == 3:
                    act.wait_ge(tile_done, T_UP + 2)
                    act.copy(glu[0:2, 0, :2 * P], bank[2][0:2, :2 * P]).then_inc(shift_row_ready, 1)
                    round_tile(T_UP + SLOTS)
                    round_tile(T_UP + SLOTS + 1)

            norm_hi(1, SHIFT_F, round_next_of_up)

            def mlp_pair(j, s, round_next, products=None):
                for half, conv in enumerate((conv_act, conv_lin)):
                    at = j + half * FC
                    act.wait_ge(tile_done, T_UP + 2 * j + half + 1)
                    product = bank[4 + 2 * s + half][:] if products is None else products[:, half]
                    act.activation(conv[:, s], product, ACT.Identity,
                                   scale=cols[:, bass.ds(at + C_WCONV + 2 * 2 * FC, 1)],
                                   bias=cols[:, bass.ds(at + C_BCONV, 1)]).then_inc(conv_begun, 1)
                    round_next(2 * s + half)
                    if half == 0:
                        act.wait_ge(conv_done, 2 * j + 1 + 4)
                        act.activation(conv_act[:, s], conv_act[:, s], ACT.Silu).then_inc(silu_done, 1)
                act.wait_ge(glu_ready, j + 1)
                act.copy(g_hi[:, bass.ds(j, 1)].rearrange("p a t -> p (a t)"), glu[:, s]).then_inc(g_hi_ready, 1)

            def round_down(n, landed):
                act.wait_ge(raw_landed[n % 2 * 2], landed)
                act.copy(down_slot(w_hi, n), down_slot(raw, n)).then_inc(hi_ready, 1)

            def mlp_pairs(i, first):
                def round_next(s):
                    act.wait_ge(raw_landed[s], 16 * (i + T_UP // SLOTS + 2))
                    act.copy(part_slot(w_hi, s), raw_slot(s)).then_inc(hi_ready, 1)

                for s in range(2):
                    if first and s == 0:
                        act.wait_ge(shifted_ready, 2)
                        for half in range(2):
                            act.wait_ge(first_scaled, WC + half + 1)
                            act.activation(squares[:, half], squares[:, half], ACT.Identity,
                                           bias=shifted[:, 1, half:half + 1]).then_inc(pair_shifted, 1)
                        act.wait_ge(pair_shifted, 2)
                        act.wait_ge(tile_done, T_UP + SLOTS)
                        mlp_pair(0, 0, lambda n: round_next(n + 2), squares)
                    else:
                        mlp_pair(2 * i + s, s, (lambda n: None) if first else round_next)

            mlp_pairs(0, True)
            with act.Fori(1, FC // 2 - 1) as i:
                mlp_pairs(i, False)
            for s in range(2):
                mlp_pair(FC - 2 + s, s, lambda n: round_down(n // 2, 16 * (T_DOWN // SLOTS + 1)) if n % 2 else None)

            def down_chunk(c, s):
                for half in range(2):
                    act.wait_ge(tile_done, T_DOWN + 2 * c + half + 1)
                    round_down(half, 16 * (c + T_DOWN // SLOTS + 2))
                act.wait_ge(down_added, c + 1 + 2)
                act.wait_ge(square_added, 2 * KC + c + 1)
                act.activation(squares[:, s], x[:, bass.ds(c, 1)].rearrange("p a t -> p (a t)"), ACT.Square) \
                    .then_inc(squared, 1)

            with act.Fori(0, KC // 2 - 1) as i:
                for s in range(2):
                    down_chunk(2 * i + s, s)
            down_chunk(KC - 2, 0)
            act.wait_ge(squared, 3 * KC - 1)
            for c in POOL_OUT:
                act.activation(x[:, c], x[:, c], ACT.Copy, scale=cols[:, C_GFIN + c:C_GFIN + c + 1]) \
                    .then_inc(scaled_hi, 1)
            act.wait_ge(square_added, 3 * KC)
            for half in range(2):
                tokens, tiles_of_half = slice(half * HALF, (half + 1) * HALF), slice(2 * half, 2 * half + 2)
                act.wait_ge(half_added, half + 1)
                act.activation(squares[:, 1, tokens], x[:, KC - 1, tokens], ACT.Square).then_inc(half_squared, 1)
                act.wait_ge(mean_ready, 3 + half)
                act.activation(small[:, 1, tiles_of_half], small[:, 0, tiles_of_half], ACT.Sqrt).then_inc(root_ready, 1)
                act.wait_ge(rstd_spread, 2 * TT + 2 * (half + 1))
                act.copy(rstd[:, tokens], bank[SPREAD_BANKS[half]][:, tokens]).then_inc(rstd_ready, 1)

        @block.vector
        def _(dve):
            order = [0]

            def then(ins):
                order[0] += 1
                ins.then_inc(dve_order, 1)
                dve.wait_ge(dve_order, order[0])

            def add_square(slot, at):
                dve.wait_ge(squared, at)
                dve.tensor_tensor(sum_sq[:], sum_sq[:], squares[:, slot], ALU.add).then_inc(square_added, 1)
                dve.wait_ge(square_added, at + 2)

            def spread_rstd(n, stat_bank):
                dve.wait_ge(stats_done, n + 1)
                dve.tensor_scalar(small[:, 0], bank[stat_bank][:, 0:TT], 1.0 / D_MODEL, EPS, ALU.mult, ALU.add) \
                    .then_inc(mean_ready, 1)
                dve.wait_ge(root_ready, n + 1)
                then(dve.reciprocal(small[:, 6], small[:, 1]))
                if n:
                    dve.wait_ge(rstd_spread, TT * n)
                for t in range(TT):
                    dve.tensor_scalar(diag[:, t * P:(t + 1) * P], ident[:], small[:, 6, t:t + 1], None, ALU.mult) \
                        .then_inc(diag_ready, 1)

            def norm_chunks(n, shift, between=None):
                dve.wait_ge(rstd_ready, n + 1)
                for c in range(KC + 1):
                    if c < KC:
                        dve.scalar_tensor_tensor(out=work[:, c % 2], in0=x[:, c], scalar=gain[:, n, c:c + 1],
                                                 in1=rstd[:], op0=ALU.mult, op1=ALU.mult) \
                            .then_inc(normed, 1)
                    if c:
                        dve.wait_ge(h_hi_ready, n * KC + c)
                        dve.scalar_tensor_tensor(out=h_lo[:, c - 1], in0=work[:, (c - 1) % 2],
                                                 scalar=mod[:, shift + c - 1:shift + c],
                                                 in1=h_hi[:, c - 1].bitcast(F32), op0=ALU.add, op1=ALU.subtract) \
                            .then_inc(h_ready, 1)
                        dve.wait_ge(h_ready, n * KC + c)
                    if c == 2 and between:
                        between()

            def split_shift(n, shift):
                then(dve.tensor_copy(shift_parts[:, n, :, 0], mod[:, shift:shift + KC]))
                dve.tensor_tensor(shift_parts[:, n, :, 1], mod[:, shift:shift + KC],
                                  shift_parts[:, n, :, 0].bitcast(F32), ALU.subtract).then_inc(shift_ready, 1)

            def sum_mod_half(n):
                wait_mod_landed(dve, n)
                group = n // 2
                acc = mod_acc[:, group % ACCS]
                for r in range(4):
                    k = n % 2 * 4 + r
                    w = mod_half(n)[:, r]
                    if k == 0:
                        then(dve.tensor_scalar(acc, w, c_act[:, 0:1], None, ALU.mult))
                        continue
                    ins = dve.scalar_tensor_tensor(out=acc, in0=w, scalar=c_act[:, k:k + 1], in1=acc,
                                                   op0=ALU.mult, op1=ALU.add)
                    if r < 3:
                        then(ins)
                ins.then_inc(mod_half_summed, 1)
                dve.wait_ge(mod_half_summed, summed(n))

            dve.sem_inc(square_added, 2)
            dve.sem_inc(scores_masked, 2)
            dve.sem_inc(attn_ready, 1)
            dve.sem_inc(branch_read, 2)
            dve.sem_inc(mixed_in, 4)
            dve.sem_inc(conv_done, 4)
            dve.sem_inc(down_added, 2)
            dve.wait_ge(c_ready, 1)
            for n in (n for n in range(EARLY) if n != ROW_HALF):
                sum_mod_half(n)
            dve.wait_ge(mod_in_bank, EARLY // 2)
            then(dve.tensor_tensor(mod[:, SCALE_M:SCALE_M + KC], bank[7][:, SCALE_M:SCALE_M + KC],
                                   cols[:, C_BMOD + SCALE_M:C_BMOD + SCALE_M + KC], ALU.add))
            dve.scalar_tensor_tensor(out=gain[:, 0], in0=mod[:, SCALE_M:SCALE_M + KC], scalar=1.0,
                                     in1=cols[:, C_GMIX:C_GMIX + KC], op0=ALU.add, op1=ALU.mult).then_inc(mod_ready, 1)
            dve.wait_ge(mod_ready, 1)
            for c in range(KC):
                dve.wait_ge(scaled_hi, c + 1)
                dve.scalar_tensor_tensor(out=h_lo[:, c], in0=x[:, c], scalar=gain[:, 0, c:c + 1],
                                         in1=h_hi[:, c].bitcast(F32), op0=ALU.mult, op1=ALU.subtract) \
                    .then_inc(scaled_ready, 1)

            def first_over_rms(n, source, to):
                if n == WC - 1:
                    dve.wait_ge(tile_done, T_VS)
                else:
                    dve.wait_ge(first_done, n + 1 - (n >= WC))
                dve.tensor_tensor(to, source[:], rstd[:], ALU.mult).then_inc(first_scaled, 1)

            for n in range(EARLY, 2 * EARLY):
                sum_mod_half(n)
            dve.wait_ge(consts_built, 2)
            spread_rstd(0, 2)
            dve.wait_ge(mod_in_bank, EARLY)
            then(dve.tensor_tensor(mod[:, SHIFT_M:SHIFT_M + KC], bank[7][:, SHIFT_M:SHIFT_M + KC],
                                   cols[:, C_BMOD + SHIFT_M:C_BMOD + SHIFT_M + KC], ALU.add))
            split_shift(0, SHIFT_M)
            dve.wait_ge(rstd_ready, 1)
            for c in range(WC - 1):
                first_over_rms(c, bank[Q_BANKS[c]], qT[:, c])
            norm_chunks(0, SHIFT_M, lambda: first_over_rms(3, bank[Q_BANKS[3]], qT[:, 3]))
            dve.wait_ge(shift_in_bank, 1)
            dve.tensor_scalar(shifted[:, 0], bank[6][:, 0:WC], HEAD_DIM ** -0.5, None, ALU.mult) \
                .then_inc(shifted_ready, 1)
            dve.memset(sum_sq[:], 0.0).then_inc(mod_ready, 1)

            def vs_mean_squares():
                for n in range(TT):
                    dve.wait_ge(vs_ready, n + 1)
                    then(dve.tensor_tensor_reduce(work[:, 0], vs[:, n], vs[:, n], 1.0, 0.0, ALU.mult, ALU.add,
                                                  small[:, 7, n:n + 1]))
                dve.tensor_scalar(small[:, 2], small[:, 7], 1.0 / WIDTH, EPS, ALU.mult, ALU.add) \
                    .then_inc(vs_mean_ready, 1)

            def vs_norm():
                dve.wait_ge(vs_root_ready, 1)
                then(dve.reciprocal(small[:, 2], small[:, 3]))
                dve.wait_ge(sgu_landed, 64)
                for n in range(TT):
                    dve.scalar_tensor_tensor(out=vs[:, n], in0=vs[:, n], scalar=small[:, 2, n:n + 1], in1=g_row[:],
                                             op0=ALU.mult, op1=ALU.mult).then_inc(vs_normed, 1)

            def sum_late_pair(pair):
                last = [None, None]

                def build_on_last(which):
                    if last[which]:
                        dve.wait_ge(*last[which])

                for half in range(2):
                    for r in range(4):
                        k = half * 4 + r
                        for which in range(2):
                            n = 2 * EARLY + 4 * pair + 2 * half + which
                            acc, w = mod_acc[:, which], mod_half(n)[:, r]
                            if r == 0:
                                wait_mod_landed(dve, n)
                            build_on_last(which)
                            if k == 0:
                                ins = dve.tensor_scalar(acc, w, c_act[:, 0:1], None, ALU.mult)
                            else:
                                ins = dve.scalar_tensor_tensor(out=acc, in0=w, scalar=c_act[:, k:k + 1], in1=acc,
                                                               op0=ALU.mult, op1=ALU.add)
                            if r == 3:
                                ins.then_inc(mod_half_summed, 1)
                                last[which] = (mod_half_summed, summed(n))
                            else:
                                order[0] += 1
                                ins.then_inc(dve_order, 1)
                                last[which] = (dve_order, order[0])
                for which in range(2):
                    build_on_last(which)
                    order[0] += 1
                    dve.transpose(mod_acc[:, 2 + which], mod_acc[:, which]).then_inc(dve_order, 1)
                    last[which] = (dve_order, order[0])
                for which in range(2):
                    build_on_last(which)
                    dve.tensor_reduce(partial[:, 2 * pair + which],
                                      mod_acc[:, 2 + which].rearrange("p (b i) -> p b i", i=BLOCK),
                                      mybir.AxisListType.X, ALU.add).then_inc(late_summed, 1)

            for pair in range(LATE // 2):
                sum_late_pair(pair)
                if pair == 0:
                    vs_mean_squares()
                if pair == 2:
                    vs_norm()
            for c in range(WC):
                dve.wait_ge(spatial_done, c + 1)
                dve.tensor_tensor(mix[:, c].rearrange("p (n i) -> p n i", i=P),
                                  bank[c][:].rearrange("p (n i) -> p n i", i=P),
                                  b_row[:, c:c + 1].broadcast_to([P, TT, P]), ALU.add).then_inc(mix_ready, 1)
            dve.wait_ge(mix_ready, WC)
            def stage_head(p, e):
                own, other = slice(64 * e, 64 * e + 64), slice(64 - 64 * e, 128 - 64 * e)
                dve.wait_ge(head_hi, 4 * p + 2 * e + 1)
                dve.tensor_tensor(q_parts[other, e], qT[own, bass.ds(p, 1)].rearrange("p a t -> p (a t)"),
                                  q_parts[own, e].bitcast(F32), ALU.subtract).then_inc(head_staged, 1)
                dve.wait_ge(head_hi, 4 * p + 2 * e + 2)
                dve.tensor_copy(k_twice[other, e], k_twice[own, e]).then_inc(head_staged, 1)
                dve.tensor_tensor(k_lo[own], kT[own, bass.ds(p, 1)].rearrange("p a t -> p (a t)"),
                                  k_twice[own, e].bitcast(F32), ALU.subtract).then_inc(head_staged, 1)

            for c in range(WC):
                if c == WC - 1:
                    for e in range(2):
                        stage_head(0, e)
                dve.wait_ge(proj_ready, 2 * WC + c + 1)
                dve.tensor_tensor(mix[:, c], mix[:, c], u[:, c % 2], ALU.mult).then_inc(gated, 1)
                dve.wait_ge(sgu_hi_ready, c + 1)
                dve.tensor_tensor(sgu_lo[:, c], mix[:, c], sgu_hi[:, c].bitcast(F32), ALU.subtract) \
                    .then_inc(sgu_ready, 1)

            dve.wait_ge(mod_in_bank, EARLY + 1)
            then(dve.tensor_tensor(mod[:, 2 * KC:], bank[7][:, 2 * KC:6 * KC],
                                   cols[:, C_BMOD + 2 * KC:C_BMOD + 6 * KC], ALU.add))
            dve.scalar_tensor_tensor(out=gain[:, 1], in0=mod[:, SCALE_F:SCALE_F + KC], scalar=1.0,
                                     in1=cols[:, C_GFFN:C_GFFN + KC], op0=ALU.add, op1=ALU.mult).then_inc(mod_ready, 1)
            split_shift(1, SHIFT_F)

            def attend_pair(p, last):
                for i in range(9):
                    if i < 8:
                        width = (i % TT + 1) * P
                        dve.wait_ge(probs_turned, 8 * p + i + 1)
                        dve.wait_ge(scores_done, 8 * p + i + 1)
                        dve.sem_inc(scores_taken, 1)
                        dve.tensor_tensor_reduce(probs[:, i % 2, :width], bank[2 + i % 2][:, :width],
                                                 mask[:, SEQ - width:], -1.0, -MASKED,
                                                 ALU.add, ALU.min, small[:, 4, i % 2:i % 2 + 1]) \
                            .then_inc(scores_masked, 1)
                    if i:
                        n = i - 1
                        width = (n % TT + 1) * P
                        dve.wait_ge(exp_done, 8 * p + n + 1)
                        dve.reciprocal(small[:, 6, n % 2:n % 2 + 1], small[:, 5, n % 2:n % 2 + 1]) \
                            .then_inc(dve_order, 1)
                        dve.wait_ge(dve_order, 8 * p + order[0] + n + 1)
                        dve.tensor_scalar(probs[:, n % 2, :width], probs[:, n % 2, :width],
                                          small[:, 6, n % 2:n % 2 + 1], None, ALU.mult).then_inc(probs_ready, 1)
                if not last:
                    stage_head(p + 1, 0)
                dve.wait_ge(attn_hi_ready, p + 1)
                dve.tensor_tensor(attn_lo[:, bass.ds(p, 1)].rearrange("p a t -> p (a t)"), bank[6][:],
                                  attn_hi[:, bass.ds(p, 1)].rearrange("p a t -> p (a t)").bitcast(F32),
                                  ALU.subtract).then_inc(attn_ready, 1)
                if not last:
                    stage_head(p + 1, 1)

            with dve.Fori(0, WC - 1) as p:
                attend_pair(p, False)
            attend_pair(WC - 1, True)
            order[0] += 8 * WC

            with dve.Fori(0, KC // SLOTS) as i:
                for s in range(SLOTS):
                    b = 2 - s % 2 * 2
                    dve.wait_ge(tile_done, T_BRANCH + SLOTS * i + s + 1)
                    dve.scalar_tensor_tensor(out=work[:, s % 2],
                                             in0=gates[:, bass.ds(2 * SLOTS * i + 2 * s, 1)].rearrange("p a t -> p (a t)"),
                                             scalar=1.0, in1=bank[b][:], op0=ALU.add, op1=ALU.mult)
                    dve.scalar_tensor_tensor(out=squares[:, s % 2],
                                             in0=gates[:, bass.ds(2 * SLOTS * i + 2 * s + 1, 1)].rearrange("p a t -> p (a t)"),
                                             scalar=1.0, in1=bank[b + 1][:], op0=ALU.add, op1=ALU.mult) \
                        .then_inc(branch_read, 1)
                    dve.wait_ge(branch_read, SLOTS * i + s + 1 + 2)
                    dve.tensor_tensor(work[:, s % 2], work[:, s % 2], squares[:, s % 2], ALU.add).then_inc(merged, 1)
                    dve.wait_ge(merged_hi, SLOTS * i + s + 1)
                    dve.scalar_tensor_tensor(out=h_lo[:, bass.ds(SLOTS * i + s, 1)].rearrange("p a t -> p (a t)"),
                                             in0=work[:, s % 2], scalar=0.5,
                                             in1=h_hi[:, bass.ds(SLOTS * i + s, 1)].rearrange("p a t -> p (a t)").bitcast(F32),
                                             op0=ALU.mult, op1=ALU.subtract).then_inc(merged_ready, 1)
                    dve.wait_ge(merged_ready, SLOTS * i + s + 1)

            with dve.Fori(0, KC // SLOTS) as i:
                for s in range(SLOTS):
                    chunk = x[:, bass.ds(SLOTS * i + s, 1)].rearrange("p a t -> p (a t)")
                    dve.wait_ge(tile_done, T_OUT + SLOTS * i + s + 1)
                    dve.scalar_tensor_tensor(out=chunk, in0=bank[4 + s][:],
                                             scalar=mod[:, bass.ds(SLOTS * i + s + GATE_M, 1)], in1=chunk,
                                             op0=ALU.mult, op1=ALU.add).then_inc(mixed_in, 1)
                    add_square(s % 2, KC + SLOTS * i + s + 1)
                    dve.wait_ge(scaled_hi, KC + SLOTS * i + s + 1)
                    dve.scalar_tensor_tensor(
                        out=g_lo[:, bass.ds(SLOTS * i + s + SCALED, 1)].rearrange("p a t -> p (a t)"),
                        in0=chunk, scalar=gain[:, 1, bass.ds(SLOTS * i + s, 1)],
                        in1=g_hi[:, bass.ds(SLOTS * i + s + SCALED, 1)].rearrange("p a t -> p (a t)").bitcast(F32),
                        op0=ALU.mult, op1=ALU.subtract).then_inc(scaled_ready, 1)
            spread_rstd(1, 6)
            norm_chunks(1, SHIFT_F)
            dve.wait_ge(shift_in_bank, 2)
            dve.tensor_copy(shifted[:, 1, 0:2], bank[2][:, 0:2]).then_inc(shifted_ready, 1)
            for half in range(2):
                first_over_rms(WC + half, bank[UP_BANKS[half]], squares[:, half])
            dve.memset(sum_sq[:], 0.0).then_inc(mod_ready, 1)

            def mlp_pairs(i, first):
                for s in range(2):
                    j = 2 * i + s
                    for half, conv in enumerate((conv_act, conv_lin)):
                        product = squares[:, half] if first and s == 0 else bank[4 + 2 * s + half]
                        dve.wait_ge(conv_begun, 2 * j + half + 1)
                        dve.scalar_tensor_tensor(out=conv[:, s, 1:], in0=product[:, :SEQ - 1],
                                                 scalar=cols[:, bass.ds(j + (half * FC + C_WCONV + 2 * FC), 1)],
                                                 in1=conv[:, s, 1:], op0=ALU.mult, op1=ALU.add).then_inc(dve_order, 1)
                        dve.wait_ge(dve_order, 4 * i + (order[0] + 2 * s + half + 1))
                        dve.scalar_tensor_tensor(out=conv[:, s, 2:], in0=product[:, :SEQ - 2],
                                                 scalar=cols[:, bass.ds(j + (half * FC + C_WCONV), 1)],
                                                 in1=conv[:, s, 2:], op0=ALU.mult, op1=ALU.add).then_inc(conv_done, 1)
                    dve.wait_ge(silu_done, j + 1)
                    dve.wait_ge(conv_done, 2 * j + 2 + 4)
                    dve.tensor_tensor(glu[:, s], conv_act[:, s], conv_lin[:, s], ALU.mult).then_inc(glu_ready, 1)
                    dve.wait_ge(g_hi_ready, j + 1)
                    dve.tensor_tensor(g_lo[:, bass.ds(j, 1)].rearrange("p a t -> p (a t)"), glu[:, s],
                                      g_hi[:, bass.ds(j, 1)].rearrange("p a t -> p (a t)").bitcast(F32),
                                      ALU.subtract).then_inc(g_ready, 1)
                    dve.wait_ge(g_ready, j + 1)

            mlp_pairs(0, True)
            with dve.Fori(1, FC // 2) as i:
                mlp_pairs(i, False)
            order[0] += 2 * FC

            def down_chunk(c, s):
                chunk = x[:, bass.ds(c, 1)].rearrange("p a t -> p (a t)")
                dve.wait_ge(tile_done, T_DOWN + 2 * c + 2)
                dve.scalar_tensor_tensor(out=chunk, in0=bank[s][:], scalar=mod[:, bass.ds(c + GATE_F, 1)], in1=chunk,
                                         op0=ALU.mult, op1=ALU.add).then_inc(down_added, 1)

            with dve.Fori(0, KC // 2 - 1) as i:
                for s in range(2):
                    down_chunk(2 * i + s, s)
                    add_square(s, 2 * KC + 2 * i + s + 1)
            down_chunk(KC - 2, 0)
            dve.wait_ge(hi_ready, T_DOWN + N_DOWN)
            dve.tensor_tensor(down_slot(w_lo, 1)[:, POOL_BLOCKS * P:], down_slot(raw, 1)[:, POOL_BLOCKS * P:],
                              down_slot(w_hi, 1)[:, POOL_BLOCKS * P:].bitcast(F32), ALU.subtract) \
                .then_inc(last_lo_ready, 1)
            add_square(0, 3 * KC - 1)
            dve.wait_ge(rstd_spread, 2 * TT)
            for half in range(2):
                tokens, tiles_of_half = slice(half * HALF, (half + 1) * HALF), slice(2 * half, 2 * half + 2)
                dve.wait_ge(half_done, half + 1)
                dve.scalar_tensor_tensor(out=x[:, KC - 1, tokens], in0=bank[DOWN_BANKS[half]][:, tokens],
                                         scalar=mod[:, GATE_F + KC - 1:GATE_F + KC], in1=x[:, KC - 1, tokens],
                                         op0=ALU.mult, op1=ALU.add).then_inc(half_added, 1)
                dve.wait_ge(stats_done, 3 + half)
                dve.tensor_scalar(small[:, 0, tiles_of_half], bank[2][:, tiles_of_half], 1.0 / D_MODEL, EPS,
                                  ALU.mult, ALU.add).then_inc(mean_ready, 1)
                dve.wait_ge(root_ready, 3 + half)
                then(dve.reciprocal(small[:, 6, tiles_of_half], small[:, 1, tiles_of_half]))
                for t in (2 * half, 2 * half + 1):
                    dve.tensor_scalar(diag[:, t * P:(t + 1) * P], ident[:], small[:, 6, t:t + 1], None, ALU.mult) \
                        .then_inc(diag_ready, 1)
                dve.wait_ge(rstd_ready, 3 + half)
                for c in (c for c in range(KC) if c not in POOL_OUT):
                    dve.scalar_tensor_tensor(out=x[:, c, tokens], in0=x[:, c, tokens],
                                             scalar=cols[:, C_GFIN + c:C_GFIN + c + 1], in1=rstd[:, tokens],
                                             op0=ALU.mult, op1=ALU.mult).then_inc(out_ready, 1)

        @block.tensor
        def _(pe):
            def product(out_ap, left, right, left_cols, right_cols, first, last):
                passes = [(0, 0), (0, 1), (1, 0)]
                for n, (a, b) in enumerate(passes):
                    ins = pe.matmul(out_ap, left[a][left_cols], right[b][right_cols],
                                    start=first and n == 0, stop=last and n == 2)
                return ins

            w, h = (w_hi, w_lo), (h_hi, h_lo)

            def block_cols(slot, k):
                return (slice(None), slice(slot * TILE + k * P, slot * TILE + (k + 1) * P))

            def chunk(k):
                return (slice(None), k)

            def token_stats(n, stat_bank):
                pe.wait_ge(square_added, KC * (n + 1) + 2)
                for t in range(TT):
                    ins = pe.matmul(bank[stat_bank][:, t:t + 1], sum_sq[:, t * P:(t + 1) * P], ones[:, 0:1],
                                    start=True, stop=True)
                ins.then_inc(stats_done, 1)

            def spread(n, spread_bank):
                for t in range(TT):
                    pe.wait_ge(diag_ready, TT * n + t + 1)
                    pe.matmul(bank[spread_bank][:, t * P:(t + 1) * P], ones[:], diag[:, t * P:(t + 1) * P],
                              start=True, stop=True).then_inc(rstd_spread, 1)

            def mod_columns(group):
                with_row = group == ROW_HALF // 2
                if with_row:
                    pe.wait_ge(mod_half_summed, summed(2 * group))
                    pe.wait_ge(mod_row_ready, 1)
                else:
                    pe.wait_ge(mod_half_summed, summed(2 * group + 1))
                for m in range(4):
                    col = bank[7][:, MOD_ORDER[group] * 4 + m:MOD_ORDER[group] * 4 + m + 1]
                    ins = pe.matmul(col, mod_acc[:, group % ACCS, m * P:(m + 1) * P], ones[:, 0:1],
                                    start=True, stop=not with_row)
                    if with_row:
                        ins = pe.matmul(col, mod_row[0:1, m * P:(m + 1) * P], ones[0:1, 0:1], start=False, stop=True)
                ins.then_inc(mod_in_bank, 1)

            pe.sem_inc(probs_turned, 2)
            pe.sem_inc(head_done, 1)
            pe.wait_ge(c_ready, 1)
            wait_mod_landed(pe, ROW_HALF)
            for r in range(4):
                ins = pe.matmul(bank[6][0:1, :], c_act[:, 4 + r:5 + r], mod_half(ROW_HALF)[:, r],
                                start=r == 0, stop=r == 3)
            ins.then_inc(mod_half_multiplied, 1)
            pe.wait_ge(consts_built, 2)
            for group in range(EARLY // 2):
                mod_columns(group)

            def weights_times_shift(n, slots, in_bank):
                for k in range(KC):
                    for part in range(2):
                        ins = pe.matmul(in_bank[0:2, :slots * P], shift_parts[:, n, k],
                                        w[part][:, :slots * TILE].rearrange("p (s k m) -> p s k m", s=slots, m=P)[:, :, k],
                                        start=k == 0 and part == 0, stop=k == KC - 1 and part == 1)
                return ins

            def turn_shift_row(n, slots, row, in_bank):
                pe.wait_ge(shift_row_ready, n + 1)
                for c in range(slots):
                    ins = pe.matmul(in_bank[:, c:c + 1], row[:, c * P:(c + 1) * P], ones[0:2, 0:1], start=True, stop=True)
                ins.then_inc(shift_in_bank, 1)

            pe.wait_ge(lo_ready, 2)
            for k in range(KC):
                pe.wait_ge(scaled_ready, k + 1)
                for t in range(2):
                    ins = product(bank[Q_BANKS[t]][:], w, h, block_cols(t, k), chunk(k), k == 0, k == KC - 1)
                    if k == KC - 1:
                        ins.then_inc(first_done, 1)
            token_stats(0, 2)
            for t in range(2, 4):
                pe.wait_ge(lo_ready, t + 1)
                for k in range(KC):
                    ins = product(bank[Q_BANKS[t]][:], w, h, block_cols(t, k), chunk(k), k == 0, k == KC - 1)
                    if k == KC - 1:
                        ins.then_inc(first_done if t == 2 else tile_done, 1)
                    elif t == 3:
                        ins.then_inc(scaled_used, 1)
                        if k == 1:
                            for group in range(EARLY // 2, EARLY):
                                mod_columns(group)
                        if k == 2:
                            spread(0, 1)
                            pe.wait_ge(shift_ready, 1)
                            weights_times_shift(0, WC, bank[6]).then_inc(tile_done, 3)

            for t in range(T_VS, T_K):
                pe.wait_ge(lo_ready, t + 1)
                for kk in range(2):
                    k = t % 4 * 2 + kk
                    if t < T_V:
                        pe.wait_ge(h_ready, k + 1)
                    for n in range(TT):
                        if t == T_VS and kk == 0 and n == 1:
                            pe.wait_ge(rstd_ready, 1)
                        if t == T_VS and kk == 0 and n in Q_BANKS:
                            pe.wait_ge(first_scaled, Q_BANKS.index(n) + 1)
                        if t == T_V and kk == 0 and n == 2:
                            pe.wait_ge(shifted_ready, 1)
                        if t == T_V and kk == 0 and n == 3:
                            pe.wait_ge(vs_ready, 1)
                        cols_w = (slice(None), slice(t % SLOTS * TILE + kk * 512, t % SLOTS * TILE + (kk + 1) * 512))
                        ins = product(bank[n if t < T_V else V_BANKS[n]][:], h, w,
                                      (slice(None), k, slice(n * P, (n + 1) * P)), cols_w,
                                      k == 0, k == KC - 1)
                ins.then_inc(tile_done, 1)
                if t == T_VS:
                    turn_shift_row(0, WC, mod_row[0:2, :], bank[6])

            for t in range(T_K, T_GATES):
                pe.wait_ge(lo_ready, t + 1)
                if t == T_K:
                    pe.wait_ge(vs_ready, TT)
                elif t == T_U:
                    pe.wait_ge(v_ready, TT)
                elif t % SLOTS >= 2:
                    pe.wait_ge(proj_ready, WC + t - T_K - 1)
                for k in range(KC):
                    ins = product(bank[(1 if t < T_U else 4) + t % 2][:], w, h, block_cols(t % SLOTS, k), chunk(k), k == 0, k == KC - 1)
                ins.then_inc(tile_done, 1)
                if t == LATE_AFTER:
                    pe.wait_ge(consts_built, 2 + P // BLOCK)
                    pe.wait_ge(late_summed, LATE)
                    for n in range(P // BLOCK):
                        ins = pe.matmul(bank[7][:, 4 * EARLY:4 * (EARLY + LATE)],
                                        select[:, (3 - n) * BLOCK:(3 - n) * BLOCK + P],
                                        partial.rearrange("p g (m n) -> p n (g m)", n=P // BLOCK)[:, n],
                                        start=n == 0, stop=n == P // BLOCK - 1)
                    ins.then_inc(mod_in_bank, 1)
                if t == T_U - 1:
                    pe.wait_ge(spatial_masked, 1)
                    pe.wait_ge(vs_normed, TT)
                    pe.wait_ge(v_ready, TT)
                    for c in range(WC):
                        if c in (1, 2):
                            pe.wait_ge(proj_ready, 2 * WC - 2 + c)
                        for e in range(2):
                            g = 2 * c + e
                            for n in range(TT):
                                ins = pe.matmul(bank[c][64 * e:64 * e + 64, n * P:(n + 1) * P],
                                                vs[:, n, g * 64:(g + 1) * 64], w_spatial[:, g, :],
                                                start=True, stop=True)
                        ins.then_inc(spatial_done, 1)

            pe.wait_ge(mix_ready, WC)
            step_units = [3, 3, 3, 3, 3, 3, 3, 3, 3, 2, 3]
            with pe.Fori(0, WC) as p:
                unit = 0
                for i in range(11):
                    for _ in range(step_units[i]):
                        j, k = unit // UNITS, unit % UNITS
                        if k == 0:
                            pe.wait_ge(lo_ready, T_GATES + 4 * p + j + 1)
                            pe.wait_ge(gate_ready, 4 * p + j + 1)
                        ins = product(bank[j % 2][:], w, h, block_cols(j, k), chunk(k), k == 0, k == KC - 1)
                        if k == KC - 1:
                            ins.then_inc(tile_done, 1)
                        unit += 1
                    if i < 8:
                        e, qb = i // TT, i % TT
                        width = (qb + 1) * P
                        rows = slice(64 * e, 64 * e + 64)
                        if qb == 0:
                            pe.wait_ge(head_staged, 6 * p + 3 * e + 3)
                        pe.wait_ge(scores_masked, 8 * p + i + 1)
                        queries = slice(qb * P, width)
                        pe.matmul(bank[2 + i % 2][:, :width], q_parts[:, e, queries], k_twice[:, e, :width],
                                  start=True, stop=False)
                        pe.matmul(bank[2 + i % 2][:, :width], q_parts[rows, e, queries], k_lo[rows, :width],
                                  start=False, stop=True).then_inc(scores_done, 1)
                    if i in (6, 10):
                        e = (i - 6) // 4
                        pe.wait_ge(probsT_ready, 8 * p + 4 * e + 4 + 2)
                        if e == 0:
                            pe.wait_ge(v_staged, p + 1)
                            pe.wait_ge(attn_ready, p + 1)
                        for kb in range(TT):
                            ins = pe.matmul(bank[6][64 * e:64 * e + 64, kb * P:], v_pair[:, kb, 64 * e:64 * e + 64],
                                            probsT[:, kb, kb * P:], start=kb == 0, stop=kb == TT - 1)
                        ins.then_inc(head_done, 1)
                    if 2 <= i < 10:
                        n, qb = i - 2, (i - 2) % TT
                        if n == 0:
                            pe.wait_ge(proj_ready, 3 * WC)
                        pe.wait_ge(probs_ready, 8 * p + n + 1)
                        pe.wait_ge(probsT_ready, 8 * p + n + 1)
                        for kb in range(qb + 1):
                            ins = pe.transpose(bank[4 + n % 2][:, kb * P:(kb + 1) * P],
                                               probs[:, n % 2, kb * P:(kb + 1) * P], ident[:])
                        ins.then_inc(probs_turned, 1)

            pe.wait_ge(scores_masked, 8 * WC + 2)
            pe.wait_ge(sgu_ready, WC)
            with pe.Fori(0, KC // SLOTS) as i:
                for s in range(SLOTS):
                    pe.wait_ge(lo_ready, T_BRANCH + SLOTS * i + s + 1)
                    pe.wait_ge(branch_read, SLOTS * i + s + 1)
                    if s == 1:
                        pe.wait_ge(gate_ready, 2 * KC + 2)
                    for k in [*range(WC, 2 * WC), *range(WC)]:
                        if s == 0 and k == 0:
                            pe.wait_ge(attn_ready, WC + 1)
                        branch = (attn_hi, attn_lo) if k < WC else (sgu_hi, sgu_lo)
                        ins = product(bank[2 - s % 2 * 2 + k // WC][:], w, branch, block_cols(s, k), chunk(k % WC),
                                      k % WC == 0, k % WC == WC - 1)
                    ins.then_inc(tile_done, 1)

            pe.wait_ge(probsT_ready, 8 * WC + 2)
            pe.wait_ge(mod_ready, 3)
            with pe.Fori(0, KC // SLOTS) as i:
                for s in range(SLOTS):
                    pe.wait_ge(lo_ready, T_OUT + SLOTS * i + s + 1)
                    pe.wait_ge(mixed_in, SLOTS * i + s + 1)
                    for k in range(KC):
                        if s == 0:
                            pe.wait_ge(merged_ready, k + 1)
                        ins = product(bank[4 + s][:], w, h, block_cols(s, k), chunk(k), k == 0, k == KC - 1)
                    ins.then_inc(tile_done, 1)
            pe.wait_ge(branch_read, KC + 2)
            pe.wait_ge(lo_ready, T_UP + 2)
            for k in range(KC):
                pe.wait_ge(scaled_ready, KC + k + 1)
                for s in range(2):
                    ins = product(bank[UP_BANKS[s]][:], w, (g_hi, g_lo), block_cols(s, k), chunk(SCALED + k),
                                  k == 0, k == KC - 1)
                    if k == KC - 1:
                        ins.then_inc(first_done, 1)
                if k == 2:
                    token_stats(1, 6)
                if k == 4:
                    spread(1, 1)
            pe.wait_ge(shift_ready, 2)
            weights_times_shift(1, 2, bank[2]).then_inc(tile_done, 2)
            pe.wait_ge(mixed_in, KC + 4)
            pe.wait_ge(lo_ready, T_UP + 4)
            for k in range(KC):
                pe.wait_ge(h_ready, KC + k + 1)
                for s in range(2, SLOTS):
                    ins = product(bank[4 + s][:], w, h, block_cols(s, k), chunk(k), k == 0, k == KC - 1)
                    if k == KC - 1:
                        ins.then_inc(tile_done, 1)
                if k == 4:
                    turn_shift_row(1, 2, glu[0:2, 0], bank[2])

            def up_tiles(i):
                for s in range(SLOTS):
                    pe.wait_ge(lo_ready, T_UP + SLOTS * i + s + 1)
                    if not (isinstance(i, int) and s < 2):
                        pe.wait_ge(conv_done, SLOTS * i + s + 1)
                    for k in range(KC):
                        ins = product(bank[4 + s][:], w, h, block_cols(s, k), chunk(k), k == 0, k == KC - 1)
                    ins.then_inc(tile_done, 1)

            up_tiles(1)
            with pe.Fori(2, FC // 2) as i:
                up_tiles(i)

            pe.wait_ge(g_ready, FC - 1)
            def down_product(c, s, first):
                pe.wait_ge(down_added, c + 1)
                for half in range(2):
                    pe.wait_ge(lo_ready, T_DOWN + 2 * c + half + 1)
                    for r in range(DOWN_UNITS):
                        k = half * DOWN_UNITS + r
                        if k == FC - 1 and first:
                            pe.wait_ge(g_ready, FC)
                        ins = product(bank[s][:], w, (g_hi, g_lo), block_cols(2 * half, r), chunk(k),
                                      k == 0, k == FC - 1)
                    ins.then_inc(tile_done, 1)

            with pe.Fori(0, KC // 2 - 1) as i:
                for s in range(2):
                    down_product(2 * i + s, s, s == 0)
            down_product(KC - 2, 0, False)

            def half_stats(half):
                pe.wait_ge(square_added, 3 * KC - 1 + 2)
                pe.wait_ge(half_squared, half + 1)
                for t in (2 * half, 2 * half + 1):
                    for source in (sum_sq, squares[:, 1]):
                        ins = pe.matmul(bank[2][:, t:t + 1], source[:, t * P:(t + 1) * P], ones[:, 0:1],
                                        start=source is sum_sq, stop=source is not sum_sq)
                ins.then_inc(stats_done, 1)

            def half_spread(half):
                for t in (2 * half, 2 * half + 1):
                    pe.wait_ge(diag_ready, 2 * TT + t + 1)
                    pe.matmul(bank[SPREAD_BANKS[half]][:, t * P:(t + 1) * P], ones[:], diag[:, t * P:(t + 1) * P],
                              start=True, stop=True).then_inc(rstd_spread, 1)

            pe.wait_ge(down_added, KC)
            for half in range(2):
                tokens = slice(half * HALF, (half + 1) * HALF)
                for k in range(FC):
                    if half == 0 and k % DOWN_UNITS == 0:
                        pe.wait_ge(lo_ready, T_DOWN + 2 * (KC - 1) + k // DOWN_UNITS + 1)
                    if half == 0 and k == DOWN_UNITS + POOL_BLOCKS:
                        pe.wait_ge(last_lo_ready, 1)
                    ins = product(bank[DOWN_BANKS[half]][:, tokens], w, (g_hi, g_lo),
                                  block_cols(k // DOWN_UNITS * 2, k % DOWN_UNITS), (slice(None), k, tokens),
                                  k == 0, k == FC - 1)
                    if half == 1 and k == STATS_AT:
                        half_stats(0)
                    if half == 1 and k == SPREAD_AT:
                        half_spread(0)
                ins.then_inc(half_done, 1)
            half_stats(1)
            half_spread(1)


def kernel(**inputs):
    import numpy as np
    import concourse.bacc as bacc
    from concourse.bass_utils import run_bass_kernel_spmd

    def a(name):
        return np.asarray(inputs[name])

    def columns(v):
        return v.reshape(-1, P).T

    def by_columns(w):
        k, n = w.shape
        return w.reshape(k // P, P, n // P, P).transpose(2, 1, 0, 3).reshape(n // P, P, k)

    def by_rows(w):
        k, n = w.shape
        return w.reshape(k // (2 * P), 2, P, n).transpose(0, 2, 1, 3).reshape(k // (2 * P), P, 2 * n)

    def alternate(one, other):
        return np.stack([one, other], axis=1).reshape(-1, *one.shape[1:])

    w_in = a("w_in")[0]
    q, k, v, u, vs = (w_in[:, n * WIDTH:(n + 1) * WIDTH] for n in range(5))
    gate_a, gate_s = (w_in[:, 5 * WIDTH + n * D_MODEL:5 * WIDTH + (n + 1) * D_MODEL] for n in range(2))
    branches = np.concatenate([by_columns(a("w_attn_br")[0]), by_columns(a("w_sgu_br")[0])], axis=2)
    w_up = a("w_up")[0]
    tiles = np.concatenate([
        by_columns(q), by_rows(vs), by_rows(v), by_columns(k), by_columns(u),
        alternate(by_columns(gate_a), by_columns(gate_s)), branches, by_columns(a("w_out")[0]),
        alternate(by_columns(w_up[:, :D_FF]), by_columns(w_up[:, D_FF:]))])
    down = by_columns(a("w_down")[0]).reshape(KC, P, 2, DOWN_TILE).transpose(0, 2, 1, 3).reshape(N_DOWN, P, DOWN_TILE)
    arrays = {
        "xT": a("x")[0].T,
        "columns": np.concatenate([columns(a(n).reshape(-1)) for n in
                                   ("c", "b_mod", "g_mix", "g_ffn", "g_final", "w_conv", "b_conv")], axis=1),
        "w_mod": a("w_mod")[0],
        "tiles": tiles,
        "down_tiles": down,
        "w_sgu": a("w_sgu_s")[0].transpose(2, 0, 1),
        "g_sgu": a("g_sgu"),
        "b_sgu": a("b_sgu_s")[0],
    }
    arrays = {name: np.ascontiguousarray(v) for name, v in arrays.items()}
    nc = bacc.Bacc("TRN2", target_bir_lowering=False, num_devices=1, dynamic_dma_scratch_size=1024)
    aps = [nc.dram_tensor(name, v.shape, mybir.dt.from_np(v.dtype), kind="ExternalInput").ap()
           for name, v in arrays.items()]
    out = nc.dram_tensor("outT", (D_MODEL, SEQ), F32, kind="ExternalOutput").ap()
    decoder_layer(nc, *aps, out)
    r = run_bass_kernel_spmd(nc, [arrays], core_ids=[0])
    return np.ascontiguousarray(r.results[0]["outT"].T)[None]
```
